# Optimizing a Trainium2 kernel written in Bass

```python
import math
import jax, jax.numpy as jnp
from jax import lax
import numpy as np

D_MODEL = 1024
BATCH = 1
SEQ = 512
DEPTH = 2

CHUNK = 64
Q_BLOCK = 128
EPS = 1e-6
D_PLE = 256
D_FF = 2816
A_HEADS = 8
A_KV_HEADS = 2
A_HEAD_DIM = 64
A_WINDOW = 128
A_WINDOW_CHUNKS = A_WINDOW // CHUNK
S5_CH = 256
S5_GROUP = 16
S5_GROUPS = S5_CH // S5_GROUP
S5_STATE = 64
C_HEADS = 8
C_HEAD_DIM = 64
C_Q_RANK = 256
C_KV_RANK = 128
IDX_HEADS = 4
IDX_DIM = 64
TOPK_MAX = 256
D_HEADS = 4
D_HEAD_DIM = 64

EV_WIDTHS = (A_HEADS * A_HEAD_DIM, A_KV_HEADS * A_HEAD_DIM, A_KV_HEADS * A_HEAD_DIM, S5_CH)
EV_IN = A_HEADS * A_HEAD_DIM + 2 * A_KV_HEADS * A_HEAD_DIM + S5_CH
EV_OUT = A_HEADS * A_HEAD_DIM + S5_CH
OD_WIDTHS = (C_Q_RANK, C_KV_RANK, IDX_DIM, IDX_HEADS,
             2 * D_HEADS * D_HEAD_DIM, 2 * D_HEADS * D_HEAD_DIM, 2 * D_HEADS * D_HEAD_DIM)
OD_IN = C_Q_RANK + C_KV_RANK + IDX_DIM + IDX_HEADS + 6 * D_HEADS * D_HEAD_DIM
OD_OUT = C_HEADS * C_HEAD_DIM + 2 * D_HEADS * D_HEAD_DIM

kernel_name = 'hybrid_streaming_encoder'

def rms_norm(x, g):
    xf = x.astype(jnp.float32)
    y = xf * lax.rsqrt(jnp.mean(xf * xf, axis=-1, keepdims=True) + EPS)
    return (y * g.astype(jnp.float32)).astype(x.dtype)

def swiglu(h, w_gate, w_up, w_down):
    return (jax.nn.silu(h @ w_gate) * (h @ w_up)) @ w_down

def split_cols(z, widths):
    out, start = [], 0
    for w in widths:
        out.append(z[..., start:start + w])
        start += w
    return out

def to_blocks(a):
    b, t = a.shape[:2]
    return jnp.moveaxis(a.reshape(b, t // Q_BLOCK, Q_BLOCK, *a.shape[2:]), 1, 0)

def from_blocks(a):
    nb, b, qb = a.shape[:3]
    return jnp.moveaxis(a, 0, 1).reshape(b, nb * qb, *a.shape[3:])

def sliding_window_sink_attention(q, k, v, sinks):
    b, t = q.shape[:2]
    nc = t // CHUNK
    g = A_HEADS // A_KV_HEADS
    qc = q.reshape(b, nc, CHUNK, A_KV_HEADS, g, A_HEAD_DIM)
    kc = k.reshape(b, nc, CHUNK, A_KV_HEADS, A_HEAD_DIM)
    vc = v.reshape(b, nc, CHUNK, A_KV_HEADS, A_HEAD_DIM)

    def band(a):
        parts = [jnp.pad(a, ((0, 0), (j, 0), (0, 0), (0, 0), (0, 0)))[:, :nc]
                 for j in range(A_WINDOW_CHUNKS - 1, -1, -1)]
        return jnp.concatenate(parts, axis=2)

    kb, vb = band(kc), band(vc)
    s = jnp.einsum('bnqkgd,bnskd->bnkgqs', qc, kb).astype(jnp.float32) * (A_HEAD_DIM ** -0.5)
    src_chunk = (jnp.arange(nc)[:, None] - (A_WINDOW_CHUNKS - 1)
                 + jnp.arange(A_WINDOW_CHUNKS * CHUNK)[None, :] // CHUNK)
    valid = (src_chunk >= 0)[None, :, None, None, None, :]
    s = jnp.where(valid, s, -jnp.inf)
    sink = sinks.astype(jnp.float32).reshape(1, 1, A_KV_HEADS, g, 1, 1)
    m = jnp.maximum(jnp.max(s, axis=-1, keepdims=True), sink)
    e = jnp.exp(s - m)
    pr = e / (jnp.sum(e, axis=-1, keepdims=True) + jnp.exp(sink - m))
    o = jnp.einsum('bnkgqs,bnskd->bnqkgd', pr.astype(v.dtype), vb)
    return o.reshape(b, t, A_HEADS * A_HEAD_DIM)

def _complex_linear_combine(earlier, later):
    a1r, a1i, b1r, b1i = earlier
    a2r, a2i, b2r, b2i = later
    return (a1r * a2r - a1i * a2i, a1r * a2i + a1i * a2r,
            a2r * b1r - a2i * b1i + b2r, a2r * b1i + a2i * b1r + b2i)

def s5_mixer(u, lam_re, lam_im, log_dt, b_re, b_im, c_re, c_im, d_skip, w_glu):
    f32 = jnp.float32
    bsz, t = u.shape[:2]
    uf = u.astype(f32).reshape(bsz, t, S5_GROUPS, S5_GROUP)
    lr, li = lam_re.astype(f32), lam_im.astype(f32)
    dt = jnp.exp(log_dt.astype(f32))[:, None]
    mag = jnp.exp(lr * dt)
    ar, ai = mag * jnp.cos(li * dt), mag * jnp.sin(li * dt)
    den = lr * lr + li * li
    zr = ((ar - 1.0) * lr + ai * li) / den
    zi = (ai * lr - (ar - 1.0) * li) / den
    br, bi = b_re.astype(f32), b_im.astype(f32)
    bbr = zr[..., None] * br - zi[..., None] * bi
    bbi = zr[..., None] * bi + zi[..., None] * br
    xr = jnp.einsum('btgp,gnp->btgn', uf, bbr)
    xi = jnp.einsum('btgp,gnp->btgn', uf, bbi)
    shape = (1, t, S5_GROUPS, S5_STATE)
    elems = (jnp.broadcast_to(ar, shape), jnp.broadcast_to(ai, shape), xr, xi)
    _, _, sr, si = lax.associative_scan(_complex_linear_combine, elems, axis=1)
    y = (jnp.einsum('btgn,gpn->btgp', sr, c_re.astype(f32))
         - jnp.einsum('btgn,gpn->btgp', si, c_im.astype(f32))
         + d_skip.astype(f32) * uf)
    y = jax.nn.gelu(y.reshape(bsz, t, S5_CH))
    y = y * jax.nn.sigmoid(y @ w_glu.astype(f32))
    return y.astype(u.dtype)

def dsa_mixer(c_q, c_kv, k_idx, w_idx, q_norm, kv_norm, w_uq, w_uk, w_uv, w_qidx):
    f32 = jnp.float32
    b, t = c_q.shape[:2]
    topk = min(TOPK_MAX, t // 4)
    cq = rms_norm(c_q, q_norm)
    ckv = rms_norm(c_kv, kv_norm)
    q = (cq @ w_uq).reshape(b, t, C_HEADS, C_HEAD_DIM)
    q_lat = jnp.einsum('bthd,rhd->bthr', q, w_uk)
    q_idx = (cq @ w_qidx).reshape(b, t, IDX_HEADS, IDX_DIM)
    w_h = w_idx * (IDX_HEADS ** -0.5)
    key_pos = jnp.arange(t)

    def block(args):
        qi, ql, wh, blk = args
        pos = blk * Q_BLOCK + jnp.arange(Q_BLOCK)
        limit = (pos // CHUNK + 1) * CHUNK
        visible = key_pos[None, :] < limit[:, None]
        score = jnp.einsum('bqhd,bsd->bqhs', qi, k_idx).astype(f32) * (IDX_DIM ** -0.5)
        score = jnp.einsum('bqhs,bqh->bqs', jax.nn.relu(score), wh.astype(f32))
        score = jnp.where(visible[None], score, -jnp.inf)
        _, idx = lax.top_k(score, topk)
        sel_ok = idx < limit[None, :, None]
        c_sel = jax.vmap(lambda c, i: c[i])(ckv, idx)
        s = jnp.einsum('bqhr,bqkr->bqhk', ql, c_sel).astype(f32) * (C_HEAD_DIM ** -0.5)
        s = jnp.where(sel_ok[:, :, None, :], s, -jnp.inf)
        pr = jax.nn.softmax(s, axis=-1).astype(c_sel.dtype)
        ctx = jnp.einsum('bqhk,bqkr->bqhr', pr, c_sel)
        return jnp.einsum('bqhr,rhd->bqhd', ctx, w_uv)

    nb = t // Q_BLOCK
    out = lax.map(block, (to_blocks(q_idx), to_blocks(q_lat), to_blocks(w_h), jnp.arange(nb)))
    return from_blocks(out).reshape(b, t, C_HEADS * C_HEAD_DIM)

def diff_attention(q, k, v, lam_q1, lam_k1, lam_q2, lam_k2, head_norm, lam_init):
    f32 = jnp.float32
    b, t = q.shape[:2]
    lam = (jnp.exp(jnp.sum(lam_q1.astype(f32) * lam_k1.astype(f32)))
           - jnp.exp(jnp.sum(lam_q2.astype(f32) * lam_k2.astype(f32))) + lam_init)
    key_pos = jnp.arange(t)

    def block(args):
        qb, blk = args
        pos = blk * Q_BLOCK + jnp.arange(Q_BLOCK)
        visible = key_pos[None, :] < ((pos // CHUNK + 1) * CHUNK)[:, None]
        s = jnp.einsum('bqhjd,bshjd->bhjqs', qb, k).astype(f32) * (D_HEAD_DIM ** -0.5)
        a = jax.nn.softmax(jnp.where(visible, s, -jnp.inf), axis=-1)
        attn = a[:, :, 0] - lam * a[:, :, 1]
        return jnp.einsum('bhqs,bshe->bqhe', attn.astype(v.dtype), v)

    nb = t // Q_BLOCK
    o = from_blocks(lax.map(block, (to_blocks(q), jnp.arange(nb))))
    o = rms_norm(o, head_norm) * (1.0 - lam_init)
    return o.reshape(b, t, D_HEADS * 2 * D_HEAD_DIM)

def setup_inputs(seed: int = 0) -> dict:
    key = jax.random.key(seed)
    ks = iter(jax.random.split(key, 40))
    n_ev = (DEPTH + 1) // 2
    n_od = DEPTH // 2
    G, N, P = S5_GROUPS, S5_STATE, S5_GROUP

    def nrm(shape, scale):
        return jax.random.normal(next(ks), shape, jnp.float32) * scale

    def gain(shape):
        return 1.0 + nrm(shape, 0.02)

    x = nrm((BATCH, SEQ, D_MODEL), 1.0)
    p = nrm((DEPTH, BATCH, SEQ, D_PLE), 1.0)
    norms = gain((DEPTH, 4, D_MODEL))
    ffn_w_gate = nrm((DEPTH, 2, D_MODEL, D_FF), D_MODEL ** -0.5)
    ffn_w_up = nrm((DEPTH, 2, D_MODEL, D_FF), D_MODEL ** -0.5)
    ffn_w_down = nrm((DEPTH, 2, D_FF, D_MODEL), D_FF ** -0.5)
    ple_w_gate = nrm((DEPTH, D_MODEL, D_MODEL), D_MODEL ** -0.5)
    ple_w_proj = nrm((DEPTH, D_PLE, D_MODEL), D_PLE ** -0.5)
    ev_w_in = nrm((n_ev, D_MODEL, EV_IN), D_MODEL ** -0.5)
    ev_w_out = nrm((n_ev, EV_OUT, D_MODEL), EV_OUT ** -0.5)
    a_sinks = nrm((n_ev, A_HEADS), 0.5)
    s5_lam_re = -0.5 + nrm((n_ev, G, N), 0.01)
    s5_lam_im = (jnp.broadcast_to(math.pi * jnp.arange(N, dtype=jnp.float32), (n_ev, G, N))
                 + nrm((n_ev, G, N), 0.01))
    s5_log_dt = jax.random.uniform(next(ks), (n_ev, G), jnp.float32, math.log(1e-3), math.log(1e-1))
    s5_b_re = nrm((n_ev, G, N, P), P ** -0.5)
    s5_b_im = nrm((n_ev, G, N, P), P ** -0.5)
    s5_c_re = nrm((n_ev, G, P, N), (2 * N) ** -0.5)
    s5_c_im = nrm((n_ev, G, P, N), (2 * N) ** -0.5)
    s5_d = nrm((n_ev, G, P), 1.0)
    s5_w_glu = nrm((n_ev, S5_CH, S5_CH), S5_CH ** -0.5)
    od_w_in = nrm((n_od, D_MODEL, OD_IN), D_MODEL ** -0.5)
    od_w_out = nrm((n_od, OD_OUT, D_MODEL), OD_OUT ** -0.5)
    c_q_norm = gain((n_od, C_Q_RANK))
    c_kv_norm = gain((n_od, C_KV_RANK))
    c_w_uq = nrm((n_od, C_Q_RANK, C_HEADS * C_HEAD_DIM), C_Q_RANK ** -0.5)
    c_w_uk = nrm((n_od, C_KV_RANK, C_HEADS, C_HEAD_DIM), C_KV_RANK ** -0.5)
    c_w_uv = nrm((n_od, C_KV_RANK, C_HEADS, C_HEAD_DIM), C_KV_RANK ** -0.5)
    c_w_qidx = nrm((n_od, C_Q_RANK, IDX_HEADS * IDX_DIM), C_Q_RANK ** -0.5)
    d_lam_q1 = nrm((n_od, D_HEAD_DIM), 0.1)
    d_lam_k1 = nrm((n_od, D_HEAD_DIM), 0.1)
    d_lam_q2 = nrm((n_od, D_HEAD_DIM), 0.1)
    d_lam_k2 = nrm((n_od, D_HEAD_DIM), 0.1)
    d_head_norm = gain((n_od, 2 * D_HEAD_DIM))
    final_norm = gain((D_MODEL,))
    return {'x': x, 'p': p, 'norms': norms, 'ffn_w_gate': ffn_w_gate, 'ffn_w_up': ffn_w_up,
            'ffn_w_down': ffn_w_down, 'ple_w_gate': ple_w_gate, 'ple_w_proj': ple_w_proj,
            'ev_w_in': ev_w_in, 'ev_w_out': ev_w_out, 'a_sinks': a_sinks,
            's5_lam_re': s5_lam_re, 's5_lam_im': s5_lam_im, 's5_log_dt': s5_log_dt,
            's5_b_re': s5_b_re, 's5_b_im': s5_b_im, 's5_c_re': s5_c_re, 's5_c_im': s5_c_im,
            's5_d': s5_d, 's5_w_glu': s5_w_glu, 'od_w_in': od_w_in, 'od_w_out': od_w_out,
            'c_q_norm': c_q_norm, 'c_kv_norm': c_kv_norm, 'c_w_uq': c_w_uq, 'c_w_uk': c_w_uk,
            'c_w_uv': c_w_uv, 'c_w_qidx': c_w_qidx, 'd_lam_q1': d_lam_q1, 'd_lam_k1': d_lam_k1,
            'd_lam_q2': d_lam_q2, 'd_lam_k2': d_lam_k2, 'd_head_norm': d_head_norm,
            'final_norm': final_norm}

def reference(x, p, norms, ffn_w_gate, ffn_w_up, ffn_w_down, ple_w_gate, ple_w_proj,
              ev_w_in, ev_w_out, a_sinks, s5_lam_re, s5_lam_im, s5_log_dt, s5_b_re, s5_b_im,
              s5_c_re, s5_c_im, s5_d, s5_w_glu, od_w_in, od_w_out, c_q_norm, c_kv_norm,
              c_w_uq, c_w_uk, c_w_uv, c_w_qidx, d_lam_q1, d_lam_k1, d_lam_q2, d_lam_k2,
              d_head_norm, final_norm):
    b, t, _ = x.shape
    h = x
    for i in range(DEPTH):
        j = i // 2
        h = h + 0.5 * swiglu(rms_norm(h, norms[i, 0]), ffn_w_gate[i, 0], ffn_w_up[i, 0], ffn_w_down[i, 0])
        hn = rms_norm(h, norms[i, 1])
        if i % 2 == 0:
            zq, zk, zv, zu = split_cols(hn @ ev_w_in[j], EV_WIDTHS)
            o_a = sliding_window_sink_attention(
                zq.reshape(b, t, A_HEADS, A_HEAD_DIM),
                zk.reshape(b, t, A_KV_HEADS, A_HEAD_DIM),
                zv.reshape(b, t, A_KV_HEADS, A_HEAD_DIM), a_sinks[j])
            o_b = s5_mixer(zu, s5_lam_re[j], s5_lam_im[j], s5_log_dt[j], s5_b_re[j], s5_b_im[j],
                           s5_c_re[j], s5_c_im[j], s5_d[j], s5_w_glu[j])
            mix = jnp.concatenate([o_a, o_b], axis=-1) @ ev_w_out[j]
        else:
            cq, ckv, kidx, widx, dq, dk, dv = split_cols(hn @ od_w_in[j], OD_WIDTHS)
            o_c = dsa_mixer(cq, ckv, kidx, widx, c_q_norm[j], c_kv_norm[j], c_w_uq[j],
                            c_w_uk[j], c_w_uv[j], c_w_qidx[j])
            lam_init = 0.8 - 0.6 * math.exp(-0.3 * i)
            o_d = diff_attention(
                dq.reshape(b, t, D_HEADS, 2, D_HEAD_DIM),
                dk.reshape(b, t, D_HEADS, 2, D_HEAD_DIM),
                dv.reshape(b, t, D_HEADS, 2 * D_HEAD_DIM),
                d_lam_q1[j], d_lam_k1[j], d_lam_q2[j], d_lam_k2[j], d_head_norm[j], lam_init)
            mix = jnp.concatenate([o_c, o_d], axis=-1) @ od_w_out[j]
        h = h + mix
        h = h + 0.5 * swiglu(rms_norm(h, norms[i, 2]), ffn_w_gate[i, 1], ffn_w_up[i, 1], ffn_w_down[i, 1])
        gate = jax.nn.sigmoid(rms_norm(h, norms[i, 3]) @ ple_w_gate[i])
        h = h + gate * (p[i] @ ple_w_proj[i])
    return rms_norm(h, final_norm)


_drawn_inputs = setup_inputs


def setup_inputs(seed=0):
    import zlib

    import numpy as np

    out = dict(_drawn_inputs(seed))
    spreads = {}
    factors = {'a_sinks': 8.0,
     's5_lam_re': 8.0,
     's5_lam_im': 2.698,
     's5_log_dt': 2.872,
     's5_b_re': 3.719,
     's5_b_im': 3.673,
     's5_c_re': 3.687,
     's5_c_im': 3.732,
     'c_q_norm': 7.604,
     'c_kv_norm': 8.0,
     'd_lam_q1': 5.243,
     'd_lam_q2': 8.0,
     'd_head_norm': 8.0,
     'final_norm': 2.837}
    for name, (base, spread) in spreads.items():
        noise = np.random.default_rng([zlib.crc32(name.encode()), seed]).standard_normal(out[name].shape)
        drawn = base * np.exp(spread * noise) if base else spread * noise
        out[name] = __import__('jax').numpy.asarray(drawn.astype(out[name].dtype))
    for name, factor in factors.items():
        out[name] = (out[name] * factor).astype(out[name].dtype)
    return out
```

```python
from contextlib import ExitStack
import math

import concourse.bass as bass
from concourse import mybir

F32 = mybir.dt.float32
F32R = mybir.dt.float32r
I32 = mybir.dt.int32
ACT = mybir.ActivationFunctionType
ALU = mybir.AluOpType
AX_X = mybir.AxisListType.X
MULT, ADD, SUB = ALU.mult, ALU.add, ALU.subtract

P = 128
D = 1024
T = 512
FF = 2816
KD = D // P
NF = FF // P
BLOCKS = 8
SLOTS = 4
AHEAD = 2
EPS = 1e-6
GROUP = 4
QB = 128
NQ = T // QB
CH = 64
HD = 64
SCALE = HD ** -0.5
HEADS = 8
MASKED = -1e30
LOWEST = -3e38
KEEP = 128
PLE_K = 2
LAM_INIT = 0.8 - 0.6 * math.exp(-0.3)
NORMS = 9

S5_G, S5_P, S5_N = 16, 16, 64
S5_J = S5_G // 2
S5_L = 8
S5_C = T // S5_L
S5_T = 2

FFN_UP, FFN_DOWN = 2 * NF, NF
EV_IN, EV_OUT, OD_IN, OD_OUT = 8, 6, 16, 8
PLE_ORDER = ("P0", "G0", "G1", "G2", "G3", "G4", "P1", "G5", "G6", "G7")
LENGTHS = (FFN_UP + FFN_DOWN, EV_IN, EV_OUT, FFN_UP + FFN_DOWN, len(PLE_ORDER),
           FFN_UP + FFN_DOWN, OD_IN, OD_OUT, FFN_UP + FFN_DOWN, len(PLE_ORDER))
STARTS = tuple(sum(LENGTHS[:i]) for i in range(len(LENGTHS) + 1))
CHUNKS = STARTS[-1]

TWO_PI = (6.28125, 0.0019340515, 1.2556659e-06)
LN2 = (0.693359375, -2.12194440e-04)
ROUND = 1.5 * 2.0 ** 23


IDX = 4
CHOOSING = tuple(m for m in range(NQ) if (m + 1) * QB > KEEP)
ROUNDS = KEEP // 8
UNITS = tuple([("d", m, i) for m in range(NQ) for i in range(4)]
              + [("c", m, i) for m in range(NQ) for i in range(HEADS)])
UNIT_OF = tuple(u for u, (kind, _, _) in enumerate(UNITS) for _ in range(2 if kind == "d" else 1))
JOBS_OF = tuple(tuple(s for s, v in enumerate(UNIT_OF) if v == u) for u in range(len(UNITS)))
SELECT_PER_UNIT = 2
NORM_AT = 32
PREP = tuple([("dv", i, 4 + i) for i in range(4)] + [("weight", 0, 0)]
             + [("q_idx", i, 1 + i) for i in range(2)]
             + [("index", CHOOSING[0] * IDX + i, 4 + i) for i in range(IDX)]
             + [("q", i, i) for i in range(4)]
             + [("index", CHOOSING[1] * IDX + i, 4 + i) for i in range(IDX)]
             + [("k", i, i) for i in range(4)]
             + [("index", CHOOSING[2] * IDX + i, 4 + i) for i in range(IDX)] + [("v", i, 4 + i) for i in range(4)])


def encoder(nc, A, out):
    with ExitStack() as ctx:
        def sb(name, shape, dt=F32):
            where = nc.sbuf_base
            return ctx.enter_context(nc.sbuf_tensor(name, shape, dt)), where

        def sem(name):
            return ctx.enter_context(nc.semaphore(name))

        h, _ = sb("h", [P, KD, T])
        x_hi, at_x = sb("x_hi", [P, KD, T], F32R)
        x_lo, at_x_lo = sb("x_lo", [P, KD, T], F32R)
        act_hi, at_hi = sb("act_hi", [P, NF * T], F32R)
        act_lo, at_lo = sb("act_lo", [P, NF * T], F32R)
        raw, _ = sb("raw", [P, SLOTS, BLOCKS, P])
        w_hi, _ = sb("w_hi", [P, SLOTS, BLOCKS, P], F32R)
        w_lo, _ = sb("w_lo", [P, SLOTS, BLOCKS, P], F32R)
        t1, at_t1 = sb("t1", [P, 2, T])
        t2, at_t2 = sb("t2", [P, 2, T])
        square, at_square = sb("square", [P, 2, T])
        rstd, at_rstd = sb("rstd", [P, T])
        std, at_std = sb("std", [P, T])
        sumsq, at_sumsq = sb("sumsq", [P, T])
        ident, _ = sb("ident", [P, P])
        ones, _ = sb("ones", [P, P])
        gains, _ = sb("gains", [P, NORMS, KD])
        eps, _ = sb("eps", [P, 1])
        s5_par, _ = sb("s5_par", [P, 3, S5_J])
        sc, _ = sb("sc", [P, 40, S5_J])
        stat, _ = sb("stat", [P, 8, 16])
        job, _ = sb("job", [P, 4, 64])
        params, _ = sb("params", [P, 16])
        tile_bytes = T * 4

        def over(name, shape, where, dt=F32):
            return nc.alloc_sbuf_tensor_at(name, shape, dt, offset=where)

        free_hi, free_lo = at_hi + 8 * tile_bytes, at_lo + 8 * tile_bytes
        pads = CH + T

        zq = over("zq", [P, 4, T], free_hi)
        k_pad = over("k_pad", [P, pads], free_hi + 8192)
        v_pad = over("v_pad", [P, pads], free_hi + 8192 + 2304)
        v_band = over("v_band", [P, 8, P], free_hi + 12800)
        prob = over("prob", [P, 2, HEADS, P], free_hi + 16896)
        s_re = over("s_re", [P, S5_J, S5_C + 1], free_hi + 25088)
        neg_row = over("neg_row", [1, P], free_hi + 25088 + 2080)
        sc_re = over("sc_re", [P, S5_J, S5_C], at_hi + 6 * tile_bytes)
        sc_im = over("sc_im", [P, S5_J, S5_C], at_hi + 7 * tile_bytes)
        u_ch = over("u_ch", [P, S5_T, T], free_lo)
        u_sc = over("u_sc", [P, S5_T, S5_L, S5_C], free_lo + 4096)
        u_grp = over("u_grp", [P, S5_G, S5_C], free_lo + 8192)
        prob_t = over("prob_t", [P, 2, HEADS, P], free_lo + 12288)
        y_grp = over("y_grp", [P, S5_G, S5_C], free_lo + 20480)
        y_ch = over("y_ch", [P, S5_T, S5_L * S5_C], free_lo + 24576)
        s_im = over("s_im", [P, S5_J, S5_C + 1], at_lo + 6 * tile_bytes)
        y_act = over("y_act", [P, S5_T, T], free_lo + 4096)
        glu = over("glu", [P, S5_T, T], free_lo + 20480)
        w_glu = over("w_glu", [P, 2, 2 * P], at_x)
        c_re = over("c_re", [P, S5_J, S5_P, S5_L], at_x + 2048)
        c_im = over("c_im", [P, S5_J, S5_P, S5_L], at_x + 6144)
        w_re = over("w_re", [P, S5_J, P], at_x + 11264)
        w_im = over("w_im", [P, S5_J, P], at_x + 15360)
        intra = over("intra", [P, S5_G, P], at_x + 19456)
        e_re = over("e_re", [P, S5_J, S5_C], at_x + 27648)
        e_im = over("e_im", [P, S5_J, S5_C], at_x + 29696)
        rot = [over(f"rot{i}", [P, S5_J, S5_C], at_t1 + i * 2048) for i in range(4)]
        decay = over("decay", [P, S5_J, S5_C], at_square)

        b_re = over("b_re", [P, S5_J, S5_P], free_lo + 20480)
        b_im = over("b_im", [P, S5_J, S5_P], free_lo + 20992)
        bb_re = over("bb_re", [P, S5_J, S5_P], free_lo + 21504)
        bb_im = over("bb_im", [P, S5_J, S5_P], free_lo + 22016)
        c0_re = over("c0_re", [P, S5_J, S5_P], free_lo + 22528)
        c0_im = over("c0_im", [P, S5_J, S5_P], free_lo + 23040)
        m_a = over("m_a", [P, 576], free_lo + 23552)
        m_b = over("m_b", [P, 576], free_lo + 25856)
        pw_re = over("pw_re", [P, S5_L + 1, S5_J], free_hi + 27680)
        pw_im = over("pw_im", [P, S5_L + 1, S5_J], free_hi + 27968)
        expo = over("expo", [P, 3 * S5_J], free_hi + 28256, I32)
        ab_re = over("ab_re", [P, S5_J, S5_P, S5_L], free_hi + 16896)
        ab_im = over("ab_im", [P, S5_J, S5_P, S5_L], free_hi + 20992)
        placed = over("placed", [P, S5_G, S5_L, S5_P], free_hi + 16896)
        taps = over("taps", [S5_P, S5_G, S5_L * S5_P], free_lo + 12288)

        dq = over("dq", [P, 4, T], free_hi)
        dk = over("dk", [P, 4, T], free_hi + 8192)
        cq = over("cq", [P, 2, T], free_hi + 16384)
        ckv = over("ckv", [P, T], free_hi + 20480)
        kidx = over("kidx", [P, T], free_hi + 22528)
        causal = over("causal", [P, T], free_hi + 24576)
        dv = over("dv", [P, 4, T], free_lo)
        kept = [over(f"kept{m}", [P, (m + 1) * QB], a)
                for m, a in zip(CHOOSING, (free_lo + 2048, free_lo + 22528, free_lo))]
        pt = over("pt", [P, 2, T], free_lo + 4096)
        w_uq = over("w_uq", [P, 2, 4 * P], free_lo + 8192)
        w_qidx = over("w_qidx", [P, 2, 2 * P], free_lo + 12288)
        w_uk = over("w_uk", [P, 4 * P], free_lo + 14336)
        w_uv = over("w_uv", [P, 4 * P], free_lo + 16384)
        q_idx = over("q_idx", [P, 2, T], free_lo + 18432)
        work = over("work", [P, T], free_lo + 24576)
        widx = over("widx", [P, T], free_lo + 26624)
        q_t = over("q_t", [P, 4, T], at_x)
        k_t = over("k_t", [P, 4, T], at_x + 8192)
        v_h = over("v_h", [P, 4, T], at_x_lo)
        v_d = over("v_d", [P, 4, T], at_x_lo + 8192)
        sm = [over(f"sm{i}", [P, T], a) for i, a in enumerate(
            (at_t1, at_t1 + 2048, at_t2, at_t2 + 2048, at_square, at_square + 2048))]
        od = over("od", [P, 4, T], free_lo + 8192)
        sq_d = over("sq_d", [P, 4, T], free_hi)
        lam_vec = over("lam_vec", [P, 4, HD], free_hi + 26624)
        lam_prod = over("lam_prod", [P, 2, HD], free_hi + 27648)

        p_raw = over("p_raw", [P, PLE_K, T], at_hi)
        p_hi = over("p_hi", [P, PLE_K, T], at_hi + 2 * tile_bytes, F32R)
        p_lo = over("p_lo", [P, PLE_K, T], at_hi + 4 * tile_bytes, F32R)
        result = over("result", [P, KD, T], free_lo)

        ps = ctx.enter_context(nc.psum_tensor("ps", [P, 8, T], F32))
        scratch_u = nc.dram_tensor("scratch_u", [S5_G * S5_P, S5_L, S5_C], F32).ap()
        scratch_y = nc.dram_tensor("scratch_y", [S5_G * S5_P, S5_L, S5_C], F32).ap()

        raw_loaded = [sem(f"raw_loaded{i}") for i in range(SLOTS)]
        hi_ready = sem("hi_ready")
        split_ready = sem("split_ready")
        chunk_used = sem("chunk_used")
        h_loaded = sem("h_loaded")
        param_loaded = sem("param_loaded")
        const_ready = sem("const_ready")
        h_ready = sem("h_ready")
        x_hi_ready = sem("x_hi_ready")
        x_lo_ready = sem("x_lo_ready")
        sum_step = sem("sum_step")
        ssq_ready = sem("ssq_ready")
        std_ready = sem("std_ready")
        rstd_ready = sem("rstd_ready")
        tile_done = sem("tile_done")
        z_ready = sem("z_ready")
        p_loaded = sem("p_loaded")
        p_hi_ready = sem("p_hi_ready")
        p_ready = sem("p_ready")
        ple_scaled = sem("ple_scaled")
        ple_gate = sem("ple_gate")
        ple_term = sem("ple_term")
        stored = sem("stored")
        out_ready = sem("out_ready")
        ffn_sems = [{n: sem(f"ffn{i}_{n}") for n in (
            "gate_scaled", "silu_done", "up_scaled", "prod_done", "act_hi_ready", "act_ready")}
            for i in range(4)]
        tab = sem("tab")
        tab_act = sem("tab_act")
        tab_pe = sem("tab_pe")
        tab_taps = sem("tab_taps")
        tab_zero = sem("tab_zero")
        tab_moved = sem("tab_moved")
        tab_in = sem("tab_in")
        pads_ready = sem("pads_ready")
        u_moved = sem("u_moved")
        u_sorted = sem("u_sorted")
        y_moved = sem("y_moved")
        s5 = {n: sem(f"s5_{n}") for n in ("x_done", "step", "state_ready", "y_done", "y_copied",
                                          "skip_done", "gelu_done", "glu_done", "gate_ready",
                                          "prod_done", "hi_ready", "lo_ready")}
        ev = {n: sem(f"ev_{n}") for n in ("v_turned", "v_ready", "scores", "max", "bias", "exp",
                                          "sink_exp", "den", "recip", "normed", "turned",
                                          "turned_copied", "pv", "hi", "lo")}
        od_s = {n: sem(f"od_{n}") for n in (
            "w_loaded", "sq_step", "ssq", "std", "rstd", "latent", "prep", "prep_read", "lam",
            "index_step", "sel_step", "const", "scores", "masked", "bias", "exp",
            "recip", "scaled", "normed", "turned", "turned_copied", "pv", "c_hi", "c_lo", "d_copied",
            "d_sq", "d_ssq", "d_std", "d_rstd", "d_out", "d_hi", "d_lo")}

        block = ctx.enter_context(nc.Block())

        def slot_of(first, j):
            return (first + j) % SLOTS

        def turn_of(first, j, i=0):
            return i + (first + j) // SLOTS

        def split_hi(act, first, j, i=0):
            if isinstance(i, int) and first + 4 * i + j >= CHUNKS:
                return
            slot = slot_of(first, j)
            act.wait_ge(raw_loaded[slot], turn_of(first, j, i) * 16 + 16)
            if not isinstance(i, int) or first + 4 * i + j >= SLOTS:
                act.wait_ge(chunk_used, i * 4 + (first + j - SLOTS + 1))
            act.activation(w_hi[:, slot], raw[:, slot], ACT.Copy).then_inc(hi_ready, 1)

        def split_lo(dve, first, j, i=0):
            if isinstance(i, int) and first + 4 * i + j >= CHUNKS:
                return
            slot = slot_of(first, j)
            dve.wait_ge(hi_ready, i * 4 + (first + j + 1))
            dve.tensor_tensor(w_lo[:, slot], raw[:, slot], w_hi[:, slot].bitcast(F32), SUB)\
               .then_inc(split_ready, 1)

        def z_base(n):
            return 0 if n == 1 else EV_IN

        def tiles_before(n, k):
            return KD * (n - 1) + k + 1

        SUM_STEPS = 2 * KD - 1

        def gained_lo(dve, n, k):
            dve.wait_ge(x_hi_ready, KD * n + k + 1)
            dve.scalar_tensor_tensor(out=x_lo[:, k], in0=h[:, k], scalar=gains[:, n, k:k + 1],
                                     in1=x_hi[:, k].bitcast(F32), op0=MULT, op1=SUB)\
               .then_inc(x_lo_ready, 1)

        def reciprocal_root(dve, n):
            dve.wait_ge(std_ready, n + 1)
            dve.reciprocal(rstd[:], std[:]).then_inc(rstd_ready, 1)
            dve.wait_ge(rstd_ready, n + 1)

        def ffn_up_dve(dve, f, n, first):
            s = ffn_sems[f]
            reciprocal_root(dve, n)

            def gate(i, b):
                dve.wait_ge(chunk_used, i * 4 + (first + 2 * b + 1))
                dve.tensor_tensor(t1[:, b], ps[:, 2 * b], rstd[:], MULT).then_inc(s["gate_scaled"], 1)

            def up(i, b):
                dve.wait_ge(chunk_used, i * 4 + (first + 2 * b + 2))
                dve.tensor_tensor(t2[:, b], ps[:, 2 * b + 1], rstd[:], MULT)\
                   .then_inc(s["up_scaled"], 1)
                dve.wait_ge(s["up_scaled"], i * 2 + (b + 1))
                dve.wait_ge(s["silu_done"], i * 2 + (b + 1))
                dve.tensor_tensor(t2[:, b], t2[:, b], t1[:, b], MULT).then_inc(s["prod_done"], 1)

            def low(i, b):
                dve.wait_ge(s["act_hi_ready"], i * 2 + (b + 1))
                span = bass.ds((i * 2 + b) * T, T)
                dve.tensor_tensor(act_lo[:, span], t2[:, b], act_hi[:, span].bitcast(F32), SUB)\
                   .then_inc(s["act_ready"], 1)

            with dve.Fori(0, NF // 2, 1) as i:
                split_lo(dve, first, AHEAD, i)
                split_lo(dve, first, AHEAD + 1, i)
                gate(i, 0)
                split_lo(dve, first, AHEAD + 2, i)
                up(i, 0)
                split_lo(dve, first, AHEAD + 3, i)
                gate(i, 1)
                low(i, 0)
                up(i, 1)
                low(i, 1)

        def down_dve(dve, n, first, steps, q, scale, after=None):
            def update(k):
                group, d = divmod(k, GROUP)
                if d < GROUP - 1:
                    dve.wait_ge(tile_done, 3 * (2 * q + group) + d + 1)
                else:
                    dve.wait_ge(chunk_used, first + steps * (group + 1))
                dve.scalar_tensor_tensor(out=h[:, k], in0=ps[:, (4, 0)[group] + d], scalar=scale,
                                         in1=h[:, k], op0=MULT, op1=ADD).then_inc(h_ready, 1)

            def low(k):
                if n < NORMS - 1:
                    gained_lo(dve, n, k)

            loops = steps // 4
            if loops > 1:
                with dve.Fori(0, loops, 1) as i:
                    for j in range(4):
                        split_lo(dve, first, AHEAD + j, i)
            else:
                loops = 0
            for j in range(4 * loops, steps):
                split_lo(dve, first, AHEAD + j)
            for j in range(steps):
                split_lo(dve, first, AHEAD + steps + j)
                if j < GROUP:
                    update(j)
                    if j:
                        low(j - 1)
            for k in range(min(steps, GROUP), KD):
                update(k)
                low(k - 1)
            if after:
                after(dve)
            low(KD - 1)

        def embedding_lo(dve, layer):
            dve.wait_ge(p_hi_ready, layer + 1)
            dve.tensor_tensor(p_lo[:], p_raw[:], p_hi[:].bitcast(F32), SUB).then_inc(p_ready, 1)

        def ple_dve(dve, layer, n, first):
            reciprocal_root(dve, n)

            def finish(k):
                dve.wait_ge(ple_gate, KD * layer + k + 1)
                dve.tensor_tensor(t2[:, k % 2], ps[:, 4 + k % GROUP], t1[:, k % 2], MULT)\
                   .then_inc(ple_term, 1)
                dve.wait_ge(ple_term, KD * layer + k + 1)
                dve.tensor_tensor(h[:, k], h[:, k], t2[:, k % 2], ADD).then_inc(h_ready, 1)

            for j, what in enumerate(PLE_ORDER):
                split_lo(dve, first, AHEAD + j)
                if what[0] == "G":
                    k = int(what[1])
                    dve.wait_ge(chunk_used, first + j + 1)
                    if k >= GROUP:
                        dve.wait_ge(chunk_used, first + PLE_ORDER.index("P1") + 1)
                    dve.tensor_tensor(t1[:, k % 2], ps[:, k % GROUP], rstd[:], MULT)\
                       .then_inc(ple_scaled, 1)
                    finish(k)
            if n + 1 < NORMS - 1:
                for k in range(KD):
                    gained_lo(dve, n + 1, k)

        def scale_tile(dve, n, first, j, bank, dsts):
            dve.wait_ge(chunk_used, first + j + 1)
            for dst, rows in dsts:
                last = dve.tensor_tensor(dst, ps[rows, bank], rstd[rows], MULT)
            last.then_inc(z_ready, 1)

        def ev_in_dve(dve, n, first):
            reciprocal_root(dve, n)
            everything = slice(0, P)
            dsts = [u_ch[:, 0], u_ch[:, 1], k_pad[:, CH:], v_pad[:, CH:]] + [zq[:, i] for i in range(4)]
            for j in range(EV_IN):
                split_lo(dve, first, AHEAD + j)
                scale_tile(dve, n, first, j, j % 4, [(dsts[j], everything)])

        DT, LRDT, LRDT8, TH, TH8, K_, RES, ACC, MAG, MAG8 = 0, 1, 2, 3, 4, 5, 7, 9, 11, 12
        SIN, SIN8, COS, COS8 = 16, 17, 18, 19
        AR, AI, UR, UI, DEN, ZR, ZI, TA, TB = range(20, 29)
        SINKS = 36
        LAM = 30

        TAB = {}

        def s5_tables_dve(dve):
            count = [0]

            def do(ins):
                count[0] += 1
                ins.then_inc(tab, 1)
                dve.wait_ge(tab, count[0])

            def row(r, n=1):
                return sc[:, r:r + n]

            def exp(dst, src, n):
                k, r, a = row(K_, n), row(RES, n), row(ACC, n)
                do(dve.tensor_scalar(k, src, 1.0 / math.log(2.0), ROUND, MULT, ADD))
                do(dve.tensor_scalar(k, k, ROUND, None, SUB))
                do(dve.tensor_scalar(k, k, -126.0, 127.0, ALU.max, ALU.min))
                do(dve.scalar_tensor_tensor(out=r, in0=k, scalar=-LN2[0], in1=src, op0=MULT, op1=ADD))
                do(dve.scalar_tensor_tensor(out=r, in0=k, scalar=-LN2[1], in1=r, op0=MULT, op1=ADD))
                do(dve.tensor_scalar(a, r, 1.0 / 5040, 1.0 / 720, MULT, ADD))
                for c in (1.0 / 120, 1.0 / 24, 1.0 / 6, 0.5, 1.0, 1.0):
                    do(dve.tensor_tensor(a, a, r, MULT))
                    do(dve.tensor_scalar(a, a, c, None, ADD))
                whole = expo[:, 0:n * S5_J].rearrange("p (a j) -> p a j", a=n)
                do(dve.tensor_scalar(whole, k, 127.0, 2.0 ** 23, ADD, MULT))
                do(dve.tensor_tensor(dst, a, whole.bitcast(F32), MULT))

            lr, li, ldt = (s5_par[:, i:i + 1] for i in range(3))
            dve.wait_ge(tab_in, 80)
            exp(row(DT), ldt, 1)
            do(dve.tensor_tensor(row(LRDT), lr, row(DT), MULT))
            do(dve.tensor_scalar(row(LRDT8), row(LRDT), float(S5_L), None, MULT))
            do(dve.tensor_tensor(row(TH), li, row(DT), MULT))
            do(dve.tensor_scalar(row(TH8), row(TH), float(S5_L), None, MULT))
            k, r = row(12, 2), row(14, 2)
            do(dve.tensor_scalar(k, row(TH, 2), 1.0 / (2 * math.pi), ROUND, MULT, ADD))
            do(dve.tensor_scalar(k, k, ROUND, None, SUB))
            do(dve.scalar_tensor_tensor(out=r, in0=k, scalar=-TWO_PI[0], in1=row(TH, 2), op0=MULT, op1=ADD))
            do(dve.scalar_tensor_tensor(out=r, in0=k, scalar=-TWO_PI[1], in1=r, op0=MULT, op1=ADD))
            do(dve.scalar_tensor_tensor(out=r, in0=k, scalar=-TWO_PI[2], in1=r, op0=MULT, op1=ADD))
            do(dve.tensor_scalar(row(SIN, 2), r, 3.1415925, -3.1415925, ALU.min, ALU.max))
            do(dve.tensor_scalar(r, r, math.pi / 2, None, ADD))
            do(dve.tensor_scalar(k, r, math.pi, -2 * math.pi, ALU.is_gt, MULT))
            do(dve.tensor_tensor(r, r, k, ADD))
            do(dve.tensor_scalar(row(COS, 2), r, 3.1415925, -3.1415925, ALU.min, ALU.max))
            TAB["angles"] = count[0]
            exp(row(MAG, 2), row(LRDT, 2), 2)
            dve.wait_ge(tab_act, 1)
            do(dve.tensor_tensor(row(AR), row(MAG), row(COS), MULT))
            do(dve.tensor_tensor(row(AI), row(MAG), row(SIN), MULT))
            do(dve.tensor_tensor(row(TA), lr, lr, MULT))
            do(dve.tensor_tensor(row(TB), li, li, MULT))
            do(dve.tensor_tensor(row(TA), row(TA), row(TB), ADD))
            do(dve.reciprocal(row(DEN), row(TA)))
            do(dve.tensor_scalar(row(UR), row(AR), -1.0, None, ADD))
            do(dve.tensor_tensor(row(TA), row(UR), lr, MULT))
            do(dve.tensor_tensor(row(TB), row(AI), li, MULT))
            do(dve.tensor_tensor(row(TA), row(TA), row(TB), ADD))
            do(dve.tensor_tensor(row(ZR), row(TA), row(DEN), MULT))
            do(dve.tensor_tensor(row(TA), row(AI), lr, MULT))
            do(dve.tensor_tensor(row(TB), row(UR), li, MULT))
            do(dve.tensor_tensor(row(TA), row(TA), row(TB), SUB))
            do(dve.tensor_tensor(row(ZI), row(TA), row(DEN), MULT))

            def cmul(o_re, o_im, a_re, a_im, b_re_, b_im_, shape, sign=1):
                n = 1
                for x in shape[1:]:
                    n *= x
                dims = " ".join("abc"[:len(shape) - 1])
                sizes = {c: v for c, v in zip("abc", shape[1:])}
                a = m_a[:, 0:n].rearrange(f"p ({dims}) -> p {dims}", **sizes)
                b = m_b[:, 0:n].rearrange(f"p ({dims}) -> p {dims}", **sizes)
                do(dve.tensor_tensor(a, a_re, b_re_, MULT))
                do(dve.tensor_tensor(b, a_im, b_im_, MULT))
                do(dve.tensor_tensor(o_re, a, b, SUB))
                do(dve.tensor_tensor(a, a_re, b_im_, MULT))
                do(dve.tensor_tensor(b, a_im, b_re_, MULT))
                do(dve.tensor_tensor(o_im, a, b, ADD))
                if sign < 0:
                    do(dve.tensor_scalar(o_im, o_im, -1.0, None, MULT))

            full = [P, S5_J, S5_P]

            def wide(r):
                return sc[:, r].unsqueeze(2).to_broadcast(full)

            cmul(bb_re[:], bb_im[:], b_re[:], b_im[:], wide(ZR), wide(ZI), full)
            do(dve.memset(pw_re[:, 0], 1.0))
            do(dve.memset(pw_im[:, 0], 0.0))
            do(dve.tensor_copy(pw_re[:, 1:2], row(AR)))
            do(dve.tensor_copy(pw_im[:, 1:2], row(AI)))
            n = 1
            while n < S5_L:
                cmul(pw_re[:, n + 1:2 * n + 1], pw_im[:, n + 1:2 * n + 1],
                     pw_re[:, 1:n + 1], pw_im[:, 1:n + 1],
                     pw_re[:, n:n + 1].to_broadcast([P, n, S5_J]),
                     pw_im[:, n:n + 1].to_broadcast([P, n, S5_J]), [P, n, S5_J])
                n *= 2
            for s in range(S5_L):
                p_re = pw_re[:, S5_L - 1 - s].unsqueeze(2).to_broadcast(full)
                p_im = pw_im[:, S5_L - 1 - s].unsqueeze(2).to_broadcast(full)
                cmul(ab_re[:, :, :, s], ab_im[:, :, :, s], bb_re[:], bb_im[:], p_re, p_im, full)
            for s in range(S5_L):
                p_re = pw_re[:, s + 1].unsqueeze(2).to_broadcast(full)
                p_im = pw_im[:, s + 1].unsqueeze(2).to_broadcast(full)
                cmul(c_re[:, :, :, s], c_im[:, :, :, s], c0_re[:], c0_im[:], p_re, p_im, full, sign=-1)
            do(dve.tensor_scalar(c0_im[:], c0_im[:], -1.0, None, MULT))
            TAB["inputs"] = count[0]
            do(dve.memset(e_re[:, :, 0], 1.0))
            do(dve.memset(e_im[:, :, 0], 0.0))
            do(dve.tensor_copy(row(UR), row(COS8)))
            do(dve.tensor_copy(row(UI), row(SIN8)))
            n = 1
            while n < S5_C:
                size = [P, S5_J, n]
                cmul(e_re[:, :, n:2 * n], e_im[:, :, n:2 * n], e_re[:, :, 0:n], e_im[:, :, 0:n],
                     sc[:, UR].unsqueeze(2).to_broadcast(size), sc[:, UI].unsqueeze(2).to_broadcast(size),
                     size)
                cmul(row(TA), row(TB), row(UR), row(UI), row(UR), row(UI), [P, 1, S5_J])
                do(dve.tensor_copy(row(UR), row(TA)))
                do(dve.tensor_copy(row(UI), row(TB)))
                n *= 2
            do(dve.tensor_copy(decay[:], sc[:, MAG8].unsqueeze(2).to_broadcast([P, S5_J, S5_C])))
            do(dve.memset(decay[:, :, 0], 0.0))

        def ev_dve(dve):
            s5_tables_dve(dve)
            steps = [0]

            def do(ins):
                steps[0] += 1
                ins.then_inc(s5["step"], 1)
                dve.wait_ge(s5["step"], steps[0])

            dve.wait_ge(s5["x_done"], 1)
            v_re = ps[:, 2].rearrange("p (j c) -> p j c", j=S5_J)
            v_im = ps[:, 3].rearrange("p (j c) -> p j c", j=S5_J)
            do(dve.tensor_tensor(rot[0][:], v_re, e_re[:], MULT))
            do(dve.tensor_tensor(rot[1][:], v_im, e_im[:], MULT))
            do(dve.tensor_tensor(rot[2][:], v_im, e_re[:], MULT))
            do(dve.tensor_tensor(rot[3][:], v_re, e_im[:], MULT))
            do(dve.tensor_tensor(rot[0][:], rot[0][:], rot[1][:], ADD))
            do(dve.tensor_tensor(rot[2][:], rot[2][:], rot[3][:], SUB))

            def biggest(m):
                dve.wait_ge(ev["scores"], m + 1)
                dve.tensor_reduce(stat[:, 0 + m % 2, 8:16],
                                  ps[:, 0:2].rearrange("p b (h k) -> p (b h) k", h=4), AX_X, ALU.max)\
                   .then_inc(ev["max"], 1)
                dve.wait_ge(ev["max"], m + 1)
                do(dve.scalar_tensor_tensor(out=stat[:, m % 2, 0:HEADS], in0=stat[:, m % 2, 8:16],
                                            scalar=-SCALE, in1=sc[:, SINKS + 1], op0=MULT, op1=ALU.min))
                dve.tensor_tensor(stat[:, 6 + m % 2, 0:HEADS], stat[:, m % 2, 0:HEADS], sc[:, SINKS],
                                  ADD).then_inc(ev["bias"], 1)

            def recip(m):
                dve.wait_ge(ev["sink_exp"], m + 1)
                dve.wait_ge(ev["exp"], HEADS * (m + 1))
                do(dve.tensor_tensor(stat[:, 2 + m % 2, 8:16], stat[:, 2 + m % 2, 0:HEADS],
                                     stat[:, 6 + m % 2, 0:HEADS], ADD))
                dve.reciprocal(stat[:, 4 + m % 2, 0:HEADS], stat[:, 2 + m % 2, 8:16])\
                   .then_inc(ev["recip"], 1)

            def out_lo(m):
                dve.wait_ge(ev["hi"], m + 1)
                span = [a[:, 0:4 * T].rearrange("p (i t) -> p i t", i=4)[:, :, m * QB:(m + 1) * QB]
                        for a in (act_hi, act_lo)]
                dve.tensor_tensor(span[1], ps[:, 6].rearrange("p (i q) -> p i q", i=4),
                                  span[0].bitcast(F32), SUB).then_inc(ev["lo"], 1)

            do(dve.tensor_scalar(sc[:, SINKS + 1], sc[:, SINKS], -1.0, None, MULT))
            biggest(0)
            flat = "p j c -> p (j c)"
            do(dve.tensor_tensor_scan(sc_re[:].rearrange(flat), decay[:].rearrange(flat),
                                      rot[0][:].rearrange(flat), 0.0, MULT, ADD))
            do(dve.tensor_tensor_scan(sc_im[:].rearrange(flat), decay[:].rearrange(flat),
                                      rot[2][:].rearrange(flat), 0.0, MULT, ADD))
            recip(0)
            do(dve.tensor_tensor(rot[0][:], sc_re[:], e_re[:], MULT))
            do(dve.tensor_tensor(rot[1][:], sc_im[:], e_im[:], MULT))
            do(dve.tensor_tensor(rot[2][:], sc_re[:], e_im[:], MULT))
            do(dve.tensor_tensor(rot[3][:], sc_im[:], e_re[:], MULT))
            dve.wait_ge(pads_ready, 6)
            dve.tensor_tensor(s_re[:, :, 1:], rot[0][:], rot[1][:], SUB).then_inc(s5["state_ready"], 1)
            dve.tensor_tensor(s_im[:, :, 1:], rot[2][:], rot[3][:], ADD).then_inc(s5["state_ready"], 1)
            biggest(1)
            recip(1)
            out_lo(0)
            for m in range(1, NQ):
                if m + 1 < NQ:
                    biggest(m + 1)
                    recip(m + 1)
                out_lo(m)
            dve.wait_ge(y_moved, 48)
            for t in range(S5_T):
                dve.scalar_tensor_tensor(
                    out=y_act[:, t].rearrange("p (c s) -> p c s", s=S5_L),
                    in0=u_ch[:, t].rearrange("p (c s) -> p c s", s=S5_L),
                    scalar=params[:, t:t + 1],
                    in1=y_ch[:, t].rearrange("p (s c) -> p c s", s=S5_L),
                    op0=MULT, op1=ADD).then_inc(s5["skip_done"], 1)
            for t in range(S5_T):
                dve.wait_ge(s5["gate_ready"], t + 1)
                dve.tensor_tensor(glu[:, t], glu[:, t], y_act[:, t], MULT).then_inc(s5["prod_done"], 1)
            for t in range(S5_T):
                dve.wait_ge(s5["hi_ready"], t + 1)
                span = slice((4 + t) * T, (5 + t) * T)
                dve.tensor_tensor(act_lo[:, span], glu[:, t], act_hi[:, span].bitcast(F32), SUB)\
                   .then_inc(s5["lo_ready"], 1)

        def od_in_dve(dve, n, first):
            reciprocal_root(dve, n)
            half, whole = slice(0, HD), slice(0, P)
            for j in range(OD_IN):
                split_lo(dve, first, AHEAD + j)
                if j < 2:
                    dsts = [(cq[:, j], whole)]
                elif j == 2:
                    dsts = [(ckv[:], whole)]
                elif j == 3:
                    rows = slice(HD, HD + IDX)
                    dsts = [(kidx[0:HD], half), (kidx[HD:P], half), (widx[rows], rows)]
                else:
                    dsts = [((dq, dk, dv)[j // 4 - 1][:, j % 4], whole)]
                scale_tile(dve, n, first, j, j % 4, dsts)
                if j == 8:
                    dve.wait_ge(od_s["std"], 2)
                    for i in range(2):
                        dve.reciprocal(sm[3 + i][:], sm[3 + i][:]).then_inc(od_s["rstd"], 1)
                    dve.wait_ge(od_s["rstd"], 2)
                    for i, x in enumerate((cq[:, 0], cq[:, 1], ckv[:])):
                        dve.scalar_tensor_tensor(out=x, in0=x, scalar=params[:, 2 + i:3 + i],
                                                 in1=sm[3 + i // 2][:], op0=MULT, op1=MULT)\
                           .then_inc(od_s["latent"], 1)

        def od_dve(dve):
            od_in_dve(dve, 5, STARTS[6])
            dve.wait_ge(od_s["w_loaded"], 16 * 5)
            dve.tensor_tensor(lam_prod[:], lam_vec[:, 0:4:2], lam_vec[:, 1:4:2], MULT)\
               .then_inc(od_s["lam"], 1)
            dve.wait_ge(od_s["lam"], 1)
            dve.tensor_reduce(sc[:, LAM, 0:2], lam_prod[:], AX_X, ADD).then_inc(od_s["lam"], 1)
            dve.wait_ge(od_s["lam"], 3)
            dve.scalar_tensor_tensor(out=sc[:, LAM, 2:3], in0=sc[:, LAM, 1:2], scalar=-LAM_INIT,
                                     in1=sc[:, LAM, 0:1], op0=ADD, op1=SUB).then_inc(od_s["lam"], 1)
            dve.tensor_scalar(sc[:, LAM, 3:4], params[:, 5:6], 1.0 - LAM_INIT, None, MULT)\
               .then_inc(od_s["lam"], 1)
            dve.wait_ge(od_s["lam"], 5)

            step = 0
            for b, m in enumerate(CHOOSING):
                keys = (m + 1) * QB
                for i in range(IDX):
                    dve.wait_ge(od_s["prep_read"], PREP.index(("index", m * IDX + i, 4 + i)) + 1)
                    if i:
                        dve.wait_ge(od_s["index_step"], step)
                    weight = stat[:, 6, m * IDX + i:m * IDX + i + 1]
                    dve.scalar_tensor_tensor(
                        out=kept[b][:], in0=sm[i][:, 0:keys], scalar=weight,
                        in1=kept[b][:] if i else causal[:, T - keys:], op0=MULT, op1=ADD).then_inc(od_s["index_step"], 1)
                    step += 1

            chosen = [0]

            def do(ins):
                chosen[0] += 1
                ins.then_inc(od_s["sel_step"], 1)
                dve.wait_ge(od_s["sel_step"], chosen[0])

            def select(number):
                if number >= ROUNDS * len(CHOOSING):
                    return
                b, at = divmod(number, ROUNDS)
                keys = (CHOOSING[b] + 1) * QB
                scores, rest, pre = kept[b][:], work[:, 0:keys], widx[:, 0:keys]
                top = stat[:, 7, 0:8]
                src = rest if at else scores
                if number == 0:
                    dve.wait_ge(od_s["index_step"], len(CHOOSING) * IDX)
                do(dve.max(out=top, in_=src))
                if at < ROUNDS - 1:
                    do(dve.match_replace(out=rest, in_to_replace=top, in_values=src,
                                         imm_value=LOWEST))
                    return
                last, count = stat[:, 7, 7:8], stat[:, 7, 8:9]
                do(dve.tensor_scalar(rest, scores, last, 0.0, ALU.is_gt, ADD, accum_out=count))
                do(dve.tensor_scalar(scores, scores, last, None, ALU.is_equal))
                do(dve.tensor_scalar(count, count, -1.0, float(KEEP), MULT, ADD))
                do(dve.tensor_tensor_scan(pre, scores, scores, 0.0, ADD, ALU.max))
                do(dve.scalar_tensor_tensor(out=scores, in0=pre, scalar=count, in1=scores,
                                            op0=ALU.is_le, op1=MULT))
                do(dve.tensor_tensor(rest, rest, scores, ADD))
                do(dve.tensor_scalar(scores, rest, -MASKED, MASKED, MULT, ADD))

            def mask(u):
                kind, m, hh = UNITS[u]
                keys = (m + 1) * QB
                for s in JOBS_OF[u]:
                    dve.wait_ge(od_s["scores"], s + 1)
                    if s >= len(sm):
                        dve.wait_ge(od_s["turned"], UNIT_OF[s - len(sm)] + 1)
                    added = kept[m - CHOOSING[0]][:] if kind == "c" and m in CHOOSING \
                        else causal[:, T - keys:]
                    dve.tensor_tensor_reduce(
                        out=sm[s % len(sm)][:, 0:keys], in0=ps[:, s % 3, 0:keys], in1=added,
                        scale=1.0, scalar=LOWEST, op0=ADD, op1=ALU.max,
                        accum_out=job[:, 0, s:s + 1]).then_inc(od_s["masked"], 1)
                for s in JOBS_OF[u]:
                    dve.wait_ge(od_s["masked"], s + 1)
                    dve.tensor_scalar(job[:, 1, s:s + 1], job[:, 0, s:s + 1], -SCALE, None, MULT)\
                       .then_inc(od_s["bias"], 1)

            def recip(u):
                for s in JOBS_OF[u]:
                    dve.wait_ge(od_s["exp"], s + 1)
                    dve.reciprocal(job[:, 3, s:s + 1], job[:, 2, s:s + 1]).then_inc(od_s["recip"], 1)

            def combine(u):
                if UNITS[u][0] != "d":
                    return
                keys = (UNITS[u][1] + 1) * QB
                s, t = JOBS_OF[u]
                dve.wait_ge(od_s["recip"], t + 1)
                do(dve.tensor_tensor(job[:, 3, t:t + 1], job[:, 3, t:t + 1], sc[:, LAM, 2:3], MULT))
                dve.wait_ge(od_s["scaled"], u + 1)
                one, two = sm[s % len(sm)][:, 0:keys], sm[t % len(sm)][:, 0:keys]
                dve.scalar_tensor_tensor(out=one, in0=two, scalar=job[:, 3, t:t + 1], in1=one,
                                         op0=MULT, op1=ADD).then_inc(od_s["normed"], 1)

            def out_lo(m):
                dve.wait_ge(od_s["c_hi"], m + 1)
                span = [a[:, 0:4 * T].rearrange("p (i t) -> p i t", i=4)[:, :, m * QB:(m + 1) * QB]
                        for a in (act_hi, act_lo)]
                dve.tensor_tensor(span[1], ps[:, 5 + m % 2].rearrange("p (i q) -> p i q", i=4),
                                  span[0].bitcast(F32), SUB).then_inc(od_s["c_lo"], 1)

            mask(0)
            mask(1)
            recip(0)
            combine(0)
            for u in range(len(UNITS)):
                if u + 2 < len(UNITS):
                    mask(u + 2)
                if u + 1 < len(UNITS):
                    recip(u + 1)
                for i in range(SELECT_PER_UNIT):
                    select(SELECT_PER_UNIT * u + i)
                if u + 1 < len(UNITS):
                    combine(u + 1)
                kind, m, hh = UNITS[u]
                if kind == "c" and hh == 0 and m:
                    out_lo(m - 1)
                if u == NORM_AT + 1:
                    dve.wait_ge(od_s["d_std"], 1)
                    dve.reciprocal(sq_d[:], sq_d[:]).then_inc(od_s["d_rstd"], 1)
                    dve.wait_ge(od_s["d_rstd"], 1)
                    dve.scalar_tensor_tensor(out=od[:].rearrange("p a t -> p (a t)"),
                                             in0=od[:].rearrange("p a t -> p (a t)"),
                                             scalar=sc[:, LAM, 3:4],
                                             in1=sq_d[:].rearrange("p a t -> p (a t)"),
                                             op0=MULT, op1=MULT).then_inc(od_s["d_out"], 1)
                if u == NORM_AT + 3:
                    dve.wait_ge(od_s["d_hi"], 1)
                    dve.tensor_tensor(act_lo[:, 4 * T:8 * T], od[:].rearrange("p a t -> p (a t)"),
                                      act_hi[:, 4 * T:8 * T].bitcast(F32), SUB)\
                       .then_inc(od_s["d_lo"], 1)
            out_lo(NQ - 1)

        @block.vector
        def _(dve):
            dve.wait_ge(param_loaded, 64)
            dve.wait_ge(h_loaded, 16)
            split_lo(dve, 0, 0)
            gained_lo(dve, 0, 0)
            split_lo(dve, 0, 1)
            for k in range(1, KD):
                gained_lo(dve, 0, k)
            ffn_up_dve(dve, 0, 0, STARTS[0])
            down_dve(dve, 1, STARTS[0] + FFN_UP, NF // 2, 0, 0.5)
            ev_in_dve(dve, 1, STARTS[1])
            ev_dve(dve)
            down_dve(dve, 2, STARTS[2], EV_OUT // 2, 1, 1.0)
            ffn_up_dve(dve, 1, 2, STARTS[3])
            down_dve(dve, 3, STARTS[3] + FFN_UP, NF // 2, 2, 0.5, lambda v: embedding_lo(v, 0))
            ple_dve(dve, 0, 3, STARTS[4])
            ffn_up_dve(dve, 2, 4, STARTS[5])
            down_dve(dve, 5, STARTS[5] + FFN_UP, NF // 2, 3, 0.5)
            od_dve(dve)
            down_dve(dve, 6, STARTS[7], OD_OUT // 2, 4, 1.0)
            ffn_up_dve(dve, 3, 6, STARTS[8])
            down_dve(dve, 7, STARTS[8] + FFN_UP, NF // 2, 5, 0.5, lambda v: embedding_lo(v, 1))
            ple_dve(dve, 1, 7, STARTS[9])
            reciprocal_root(dve, 8)
            for k in range(KD):
                dve.scalar_tensor_tensor(out=result[:, k], in0=h[:, k], scalar=gains[:, 8, k:k + 1],
                                         in1=rstd[:], op0=MULT, op1=MULT).then_inc(out_ready, 1)

        @block.sync
        def _(sp):
            sp.dma_start(h[:], A["xT"].rearrange("(k p) t -> p k t", p=P)).then_inc(h_loaded, 16)
            for slot in range(SLOTS):
                sp.dma_start(raw[:, slot], A["weights"][slot]).then_inc(raw_loaded[slot], 16)
            turns = CHUNKS // SLOTS
            with sp.Fori(1, turns, 1) as i:
                for slot in range(SLOTS):
                    sp.wait_ge(split_ready, i * SLOTS + (slot - SLOTS + 1))
                    sp.dma_start(raw[:, slot], A["weights"][bass.ds(i * SLOTS + slot, 1)]
                                 .rearrange("a p b f -> (a p) b f")).then_inc(raw_loaded[slot], 16)
            for c in range(turns * SLOTS, CHUNKS):
                sp.wait_ge(split_ready, c - SLOTS + 1)
                sp.dma_start(raw[:, c % SLOTS], A["weights"][c]).then_inc(raw_loaded[c % SLOTS], 16)
            rows = out.rearrange("(k p) t -> p k t", p=P)
            for k in range(0, KD, 2):
                sp.wait_ge(out_ready, k + 2)
                sp.dma_start(rows[:, k:k + 2], result[:, k:k + 2]).then_inc(stored, 16)
            sp.wait_ge(stored, 16 * KD // 2)

        def sum_squares(pool, n):
            done = SUM_STEPS * n
            for k in range(KD):
                if n == 0:
                    pool.wait_ge(h_loaded, 16)
                else:
                    pool.wait_ge(h_ready, tiles_before(n, k))
                if k == 0:
                    if n > 0:
                        pool.wait_ge(ssq_ready, n)
                    pool.tensor_tensor(sumsq[:], h[:, 0], h[:, 0], MULT).then_inc(sum_step, 1)
                    done += 1
                    continue
                pool.tensor_tensor(square[:, k % 2], h[:, k], h[:, k], MULT).then_inc(sum_step, 1)
                pool.wait_ge(sum_step, done + 1)
                pool.tensor_tensor(sumsq[:], sumsq[:], square[:, k % 2], ADD).then_inc(sum_step, 1)
                done += 2
                pool.wait_ge(sum_step, done)

        def s5_loads(pool):
            for dst, name in ((b_re, "s5_b_re"), (b_im, "s5_b_im"), (c0_re, "s5_c_re"),
                              (c0_im, "s5_c_im")):
                pool.dma_start(dst[:], A[name]).then_inc(tab_in, 16)

        def s5_tables_pool(pool):
            pool.wait_ge(tab_pe, 4)
            pool.memset(placed[:], 0.0).then_inc(tab_zero, 1)
            pool.wait_ge(tab_zero, 1)
            pool.wait_ge(tab_taps, 1)
            flat = placed[:].rearrange("p g s q -> p g (s q)")
            for s in range(S5_L):
                pool.dma_start(flat[s::S5_L, :, s * S5_P:],
                               taps[:, :, 0:(S5_L - s) * S5_P]).then_inc(tab_moved, 16)
            pool.wait_ge(tab_moved, 16 * S5_L)
            pool.tensor_copy(intra[:].rearrange("p g (q s) -> p g q s", s=S5_L),
                             placed[:].rearrange("p g s q -> p g q s")).then_inc(tab_zero, 1)

        def ev_pool(pool):
            base = STARTS[1]
            pool.memset(k_pad[:, 0:CH], 0.0).then_inc(pads_ready, 1)
            pool.memset(v_pad[:, 0:CH], 0.0).then_inc(pads_ready, 1)
            pool.memset(neg_row[:], 0.0).then_inc(pads_ready, 1)
            pool.wait_ge(pads_ready, 3)
            pool.memset(neg_row[:, 0:CH], MASKED).then_inc(pads_ready, 1)
            pool.memset(s_re[:, :, 0:1], 0.0).then_inc(pads_ready, 1)
            pool.memset(s_im[:, :, 0:1], 0.0).then_inc(pads_ready, 1)
            pool.wait_ge(u_sorted, S5_T)
            pool.dma_start(scratch_u.rearrange("(t p) s c -> p t s c", t=S5_T), u_sc[:])\
                .then_inc(u_moved, 16)
            pool.wait_ge(u_moved, 16)
            pool.dma_start(u_grp[:], scratch_u.rearrange("(g p) s c -> (p s) g c", g=S5_G))\
                .then_inc(u_moved, 16)
            s5_tables_pool(pool)
            for m in range(NQ):
                pool.wait_ge(ev["recip"], m + 1)
                pool.tensor_tensor(prob[:, m % 2], prob[:, m % 2],
                                   stat[:, 4 + m % 2, 0:HEADS].unsqueeze(2)
                                   .to_broadcast([P, HEADS, P]), MULT).then_inc(ev["normed"], 1)
                if m == 0:
                    pool.wait_ge(s5["y_copied"], 1)
                    rows = scratch_y.rearrange("(j two p) s c -> two (p s) j c", two=2, p=S5_P)
                    for parity in range(2):
                        pool.dma_start(rows[parity], y_grp[:, S5_J * parity:S5_J * (parity + 1)])\
                            .then_inc(y_moved, 16)
                    pool.wait_ge(y_moved, 32)
                    pool.dma_start(y_ch[:], scratch_y.rearrange("(t p) s c -> p t (s c)", t=S5_T))\
                        .then_inc(y_moved, 16)

        def load_embedding(pool, layer, segment):
            pool.wait_ge(chunk_used, STARTS[segment + 1] - NF // 2 + 3)
            pool.dma_start(p_raw[:], A["pT"][layer].rearrange("(k p) t -> p k t", p=P))\
                .then_inc(p_loaded, 16)

        def od_pool(pool):
            pool.wait_ge(chunk_used, STARTS[6])
            for dst, name in ((w_uq, "w_uq"), (w_qidx, "w_qidx"), (w_uk, "w_uk"), (w_uv, "w_uv"),
                              (lam_vec, "lam_vec")):
                pool.dma_start(dst[:], A[name]).then_inc(od_s["w_loaded"], 16)
            pool.memset(causal[:], 0.0).then_inc(od_s["const"], 1)
            pool.wait_ge(od_s["const"], 1)
            pool.memset(causal[0:CH, T - CH:], MASKED).then_inc(od_s["const"], 1)
            zb = z_base(5)
            pool.wait_ge(z_ready, zb + 3)
            pool.tensor_tensor(sm[0][:], cq[:, 0], cq[:, 0], MULT).then_inc(od_s["sq_step"], 1)
            pool.tensor_tensor(sm[1][:], cq[:, 1], cq[:, 1], MULT).then_inc(od_s["sq_step"], 1)
            pool.tensor_tensor(sm[2][:], ckv[:], ckv[:], MULT).then_inc(od_s["sq_step"], 1)
            pool.wait_ge(od_s["sq_step"], 3)
            pool.tensor_tensor(sm[0][:], sm[0][:], sm[1][:], ADD).then_inc(od_s["sq_step"], 1)
            for u, (kind, m, hh) in enumerate(UNITS):
                s = JOBS_OF[u][0]
                keys = (m + 1) * QB
                pool.wait_ge(od_s["recip"], s + 1)
                pool.tensor_scalar(sm[s % len(sm)][:, 0:keys], sm[s % len(sm)][:, 0:keys],
                                   job[:, 3, s:s + 1], None, MULT).then_inc(od_s["scaled"], 1)
                if u == NORM_AT - 4:
                    pool.wait_ge(od_s["d_copied"], NQ)
                    pool.tensor_tensor(sq_d[:], od[:], od[:], MULT).then_inc(od_s["d_sq"], 1)

        @block.gpsimd
        def _(pool):
            pool.dma_start(gains[:], A["gains"]).then_inc(param_loaded, 16)
            pool.dma_start(s5_par[:], A["s5_par"]).then_inc(param_loaded, 16)
            pool.dma_start(params[:], A["params"]).then_inc(param_loaded, 16)
            pool.dma_start(sc[:, 36], A["sinks"]).then_inc(param_loaded, 16)
            pool.memset(eps[:], EPS).then_inc(const_ready, 1)
            pool.memset(ones[:], 1.0).then_inc(const_ready, 1)
            pool.memset(ident[:], 0.0).then_inc(const_ready, 1)
            pool.wait_ge(const_ready, 3)
            pool.affine_select(out=ident[:], in_=ident[:], compare_op=ALU.not_equal, fill=1.0,
                               base=0, pattern=[[-1, P]], channel_multiplier=1)\
                .then_inc(const_ready, 1)
            sum_squares(pool, 0)
            sum_squares(pool, 1)
            pool.wait_ge(chunk_used, STARTS[1])
            s5_loads(pool)
            pool.wait_ge(chunk_used, STARTS[2])
            pool.dma_start(w_glu[:], A["w_glu"]).then_inc(tab_in, 16)
            ev_pool(pool)
            sum_squares(pool, 2)
            load_embedding(pool, 0, 3)
            sum_squares(pool, 3)
            sum_squares(pool, 4)
            sum_squares(pool, 5)
            od_pool(pool)
            sum_squares(pool, 6)
            load_embedding(pool, 1, 8)
            sum_squares(pool, 7)
            sum_squares(pool, 8)

        def root(act, n):
            act.wait_ge(ssq_ready, n + 1)
            act.activation(std[:], ps[:, 3 if n in (3, 7) else 4], ACT.Sqrt, bias=eps[:, 0:1],
                           scale=1.0 / D).then_inc(std_ready, 1)

        def gained_hi(act, n, k):
            if n == 0:
                act.wait_ge(h_loaded, 16)
            else:
                act.wait_ge(h_ready, tiles_before(n, k))
            act.activation(x_hi[:, k], h[:, k], ACT.Copy, scale=gains[:, n, k:k + 1])\
               .then_inc(x_hi_ready, 1)

        def ffn_up_act(act, f, n, first):
            s = ffn_sems[f]
            root(act, n)

            def silu(tile, b):
                act.wait_ge(s["gate_scaled"], tile + 1)
                act.activation(t1[:, b], t1[:, b], ACT.Silu).then_inc(s["silu_done"], 1)

            def product_hi(tile, b):
                act.wait_ge(s["prod_done"], tile + 1)
                act.activation(act_hi[:, bass.ds(tile * T, T)], t2[:, b], ACT.Copy)\
                   .then_inc(s["act_hi_ready"], 1)

            def two_tiles(i):
                split_hi(act, first, AHEAD, i)
                split_hi(act, first, AHEAD + 1, i)
                silu(i * 2, 0)
                split_hi(act, first, AHEAD + 2, i)
                product_hi(i * 2, 0)
                split_hi(act, first, AHEAD + 3, i)
                silu(i * 2 + 1, 1)
                product_hi(i * 2 + 1, 1)

            two_tiles(0)
            with act.Fori(1, NF // 2, 1) as i:
                two_tiles(i)

        def down_act(act, n, first, steps, after=None):
            loops = steps // 4
            if loops > 1:
                with act.Fori(0, loops, 1) as i:
                    for j in range(4):
                        split_hi(act, first, AHEAD + j, i)
            else:
                loops = 0
            for j in range(4 * loops, steps):
                split_hi(act, first, AHEAD + j)
            for j in range(steps):
                split_hi(act, first, AHEAD + steps + j)
                if j < GROUP and n < NORMS - 1:
                    gained_hi(act, n, j)
            if n < NORMS - 1:
                for k in range(min(steps, GROUP), KD):
                    gained_hi(act, n, k)
            if after:
                after(act)

        def embedding_hi(act, layer):
            act.wait_ge(p_loaded, 16 * (layer + 1))
            act.activation(p_hi[:], p_raw[:], ACT.Copy).then_inc(p_hi_ready, 1)

        def ple_act(act, layer, n, first):
            root(act, n)
            for j, what in enumerate(PLE_ORDER):
                split_hi(act, first, AHEAD + j)
                if what[0] == "G":
                    k = int(what[1])
                    act.wait_ge(ple_scaled, KD * layer + k + 1)
                    act.activation(t1[:, k % 2], t1[:, k % 2], ACT.Sigmoid).then_inc(ple_gate, 1)
            if n + 1 < NORMS - 1:
                act.wait_ge(chunk_used, first + len(PLE_ORDER))
                for k in range(KD):
                    gained_hi(act, n + 1, k)

        def s5_tables_act(act):
            act.wait_ge(tab, TAB["angles"])
            act.activation(sc[:, 16:20], sc[:, 16:20], ACT.Sin).then_inc(tab_act, 1)
            for half in range(4):
                act.wait_ge(tab_pe, half + 1)
                dst = (w_re, w_im)[half // 2]
                act.activation(dst[:, 4 * (half % 2):4 * (half % 2) + 4],
                               ps[:, half].rearrange("p (j q) -> p j q", j=4), ACT.Copy)\
                   .then_inc(tab_act, 1)
            act.wait_ge(tab_pe, 5)
            act.activation(taps[:], ps[0:S5_P, 4:8].rearrange("p b (g x) -> p (b g) x", g=4),
                           ACT.Copy).then_inc(tab_taps, 1)

        def ev_in_act(act, n, first):
            root(act, n)
            for j in range(EV_IN):
                split_hi(act, first, AHEAD + j)
                if j in (2, 3):
                    act.wait_ge(z_ready, j - 1)
                    act.activation(u_sc[:, j - 2],
                                   u_ch[:, j - 2].rearrange("p (c s) -> p s c", s=S5_L), ACT.Copy)\
                       .then_inc(u_sorted, 1)

        def ev_act(act):
            s5_tables_act(act)

            def exps(m):
                act.wait_ge(ev["bias"], m + 1)
                if m >= 2:
                    act.wait_ge(ev["turned"], m - 1)
                else:
                    act.wait_ge(tab_zero, 2)
                for hh in range(HEADS):
                    act.activation(prob[:, m % 2, hh], ps[:, hh // 4, (hh % 4) * P:(hh % 4 + 1) * P],
                                   ACT.Exp, bias=stat[:, m % 2, hh:hh + 1], scale=SCALE,
                                   accum_out=stat[:, 2 + m % 2, hh:hh + 1]).then_inc(ev["exp"], 1)
                act.activation(stat[:, 6 + m % 2, 0:HEADS], stat[:, 6 + m % 2, 0:HEADS], ACT.Exp)\
                   .then_inc(ev["sink_exp"], 1)

            def turned(m):
                act.wait_ge(ev["turned"], m + 1)
                act.activation(prob_t[:, m % 2], ps[:, 4:6].rearrange("p b (h q) -> p (b h) q", h=4),
                               ACT.Copy).then_inc(ev["turned_copied"], 1)

            def out_hi(m):
                act.wait_ge(ev["pv"], m + 1)
                act.activation(act_hi[:, 0:4 * T].rearrange("p (i t) -> p i t", i=4)
                               [:, :, m * QB:(m + 1) * QB],
                               ps[:, 6].rearrange("p (i q) -> p i q", i=4), ACT.Copy)\
                   .then_inc(ev["hi"], 1)

            act.wait_ge(ev["v_turned"], 1)
            act.activation(v_band[:], ps[:, 4:6].rearrange("p b (n x) -> p (b n) x", n=4), ACT.Copy)\
               .then_inc(ev["v_ready"], 1)
            exps(0)
            turned(0)
            exps(1)
            act.wait_ge(s5["y_done"], 1)
            act.activation(y_grp[:], ps[:, 2:4].rearrange("p b (g c) -> p (b g) c", g=8), ACT.Copy)\
               .then_inc(s5["y_copied"], 1)
            out_hi(0)
            for m in range(1, NQ):
                turned(m)
                if m + 1 < NQ:
                    exps(m + 1)
                out_hi(m)
            act.wait_ge(s5["skip_done"], S5_T)
            act.activation(y_act[:], y_act[:], ACT.Gelu_apprx_tanh).then_inc(s5["gelu_done"], 1)
            for t in range(S5_T):
                act.wait_ge(s5["glu_done"], t + 1)
                if t == 0:
                    act.wait_ge(y_moved, 32)
                act.activation(glu[:, t], ps[:, t], ACT.Sigmoid).then_inc(s5["gate_ready"], 1)
            for t in range(S5_T):
                act.wait_ge(s5["prod_done"], t + 1)
                act.activation(act_hi[:, (4 + t) * T:(5 + t) * T], glu[:, t], ACT.Copy)\
                   .then_inc(s5["hi_ready"], 1)

        def block_out(act, kind, m):
            unit = UNITS.index((kind, m, 3 if kind == "d" else HEADS - 1))
            act.wait_ge(od_s["pv"], unit + 1)
            src = ps[:, 5 + m % 2].rearrange("p (i q) -> p i q", i=4)
            if kind == "d":
                act.activation(od[:, :, m * QB:(m + 1) * QB], src, ACT.Copy)\
                   .then_inc(od_s["d_copied"], 1)
            else:
                act.activation(act_hi[:, 0:4 * T].rearrange("p (i t) -> p i t", i=4)
                               [:, :, m * QB:(m + 1) * QB], src, ACT.Copy).then_inc(od_s["c_hi"], 1)

        def od_act(act):
            first = STARTS[6]
            root(act, 5)
            for j in range(OD_IN):
                split_hi(act, first, AHEAD + j)
                if j == 7:
                    act.wait_ge(od_s["ssq"], 2)
                    for i, width in enumerate((2 * P, P)):
                        act.activation(sm[3 + i][:], ps[:, 5 + i], ACT.Sqrt, bias=eps[:, 0:1],
                                       scale=1.0 / width).then_inc(od_s["std"], 1)
            act.wait_ge(od_s["lam"], 2)
            act.activation(sc[:, LAM, 0:2], sc[:, LAM, 0:2], ACT.Exp).then_inc(od_s["lam"], 1)
            for number, (kind, i, bank) in enumerate(PREP):
                act.wait_ge(od_s["prep"], number + 1)
                if kind == "weight":
                    last = act.activation(stat[:, 6, 0:NQ * IDX], ps[:, bank, 0:NQ * IDX], ACT.Copy,
                                          scale=IDX ** -0.5)
                elif kind == "index":
                    keys = (i // IDX + 1) * QB
                    if i // IDX > CHOOSING[0]:
                        act.wait_ge(od_s["index_step"], i - (CHOOSING[0] + 1) * IDX + 1)
                    last = act.activation(sm[i % IDX][:, 0:keys], ps[:, bank, 0:keys], ACT.Relu,
                                          scale=HD ** -0.5)
                else:
                    dst = {"q_idx": q_idx, "q": q_t, "k": k_t, "v": v_h, "dv": v_d}[kind]
                    last = act.activation(dst[:, i], ps[:, bank], ACT.Copy)
                last.then_inc(od_s["prep_read"], 1)

            def exps(u):
                keys = (UNITS[u][1] + 1) * QB
                for s in JOBS_OF[u]:
                    act.wait_ge(od_s["bias"], s + 1)
                    buf = sm[s % len(sm)][:, 0:keys]
                    act.activation(buf, buf, ACT.Exp, bias=job[:, 1, s:s + 1], scale=SCALE,
                                   accum_out=job[:, 2, s:s + 1]).then_inc(od_s["exp"], 1)

            def turned(u):
                keys = (UNITS[u][1] + 1) * QB
                act.wait_ge(od_s["turned"], u + 1)
                if u >= 2:
                    act.wait_ge(od_s["pv"], u - 1)
                act.activation(pt[:, u % 2, 0:keys], ps[:, 3 + u % 2, 0:keys], ACT.Copy)\
                   .then_inc(od_s["turned_copied"], 1)

            exps(0)
            exps(1)
            for u, (kind, m, hh) in enumerate(UNITS):
                if u + 2 < len(UNITS):
                    exps(u + 2)
                turned(u)
                if u and UNITS[u - 1][:2] != (kind, m):
                    block_out(act, *UNITS[u - 1][:2])
                if u == NORM_AT:
                    for i in range(4):
                        act.wait_ge(od_s["d_ssq"], i + 1)
                        act.activation(sq_d[:, i], ps[:, 7], ACT.Copy, scale=1.0 / P)\
                           .then_inc(od_s["d_sq"], 1)
                    act.wait_ge(od_s["d_sq"], 5)
                    act.activation(sq_d[:], sq_d[:], ACT.Sqrt, bias=eps[:, 0:1])\
                       .then_inc(od_s["d_std"], 1)
                if u == NORM_AT + 2:
                    act.wait_ge(od_s["d_out"], 1)
                    act.activation(act_hi[:, 4 * T:8 * T], od[:].rearrange("p a t -> p (a t)"),
                                   ACT.Copy).then_inc(od_s["d_hi"], 1)
            block_out(act, "c", NQ - 1)

        @block.scalar
        def _(act):
            act.wait_ge(param_loaded, 64)
            act.wait_ge(const_ready, 4)
            split_hi(act, 0, 0)
            gained_hi(act, 0, 0)
            split_hi(act, 0, 1)
            for k in range(1, KD):
                gained_hi(act, 0, k)
            ffn_up_act(act, 0, 0, STARTS[0])
            down_act(act, 1, STARTS[0] + FFN_UP, NF // 2)
            ev_in_act(act, 1, STARTS[1])
            ev_act(act)
            down_act(act, 2, STARTS[2], EV_OUT // 2)
            ffn_up_act(act, 1, 2, STARTS[3])
            down_act(act, 3, STARTS[3] + FFN_UP, NF // 2, lambda a: embedding_hi(a, 0))
            ple_act(act, 0, 3, STARTS[4])
            ffn_up_act(act, 2, 4, STARTS[5])
            down_act(act, 5, STARTS[5] + FFN_UP, NF // 2)
            od_act(act)
            down_act(act, 6, STARTS[7], OD_OUT // 2)
            ffn_up_act(act, 3, 6, STARTS[8])
            down_act(act, 7, STARTS[8] + FFN_UP, NF // 2, lambda a: embedding_hi(a, 1))
            ple_act(act, 1, 7, STARTS[9])
            root(act, 8)

        def in_chunk(pe, first, j, bank, i=0, n=None, rhs=(x_hi, x_lo)):
            slot = slot_of(first, j)
            pe.wait_ge(split_ready, i * 4 + (first + j + 1))
            if n:
                pe.wait_ge(h_ready, tiles_before(n, GROUP))
            for k in range(KD):
                if n is not None:
                    pe.wait_ge(x_lo_ready, KD * n + k + 1)
                for part, (w, x) in enumerate(((w_hi, rhs[0]), (w_hi, rhs[1]), (w_lo, rhs[0]))):
                    last = pe.matmul(ps[:, bank], w[:, slot, k], x[:, k],
                                     start=(k == 0 and part == 0), stop=(k == KD - 1 and part == 2))
            last.then_inc(chunk_used, 1)

        def down_chunk(pe, first, j, group, start, stop_, rhs_hi, rhs_lo, i=0, whole=True):
            slot = slot_of(first, j)
            pe.wait_ge(split_ready, i * 4 + (first + j + 1))
            for d in range(GROUP):
                for row in range(2):
                    b = row * GROUP + d
                    for part, (w, x) in enumerate(((w_hi, rhs_hi), (w_hi, rhs_lo), (w_lo, rhs_hi))):
                        last = pe.matmul(ps[:, (4, 0)[group] + d], w[:, slot, b], x(row),
                                         start=(start and row == 0 and part == 0),
                                         stop=(stop_ and row == 1 and part == 2))
                if stop_ and d < GROUP - 1 and whole:
                    last.then_inc(tile_done, 1)
            last.then_inc(chunk_used, 1)

        def squares(pe, n):
            pe.wait_ge(sum_step, SUM_STEPS * (n + 1))
            pe.matmul(ps[:, 3 if n in (3, 7) else 4], ones[:], sumsq[:], start=True, stop=True)\
              .then_inc(ssq_ready, 1)

        def ffn_up_pe(pe, f, n, first):
            s = ffn_sems[f]
            for j in range(4):
                in_chunk(pe, first, j, j, n=n if j == 0 else None)
                if j == 0:
                    squares(pe, n)
            with pe.Fori(1, NF // 2, 1) as i:
                for j in range(4):
                    tile = i * 2 + j // 2
                    pe.wait_ge(s["up_scaled"] if j % 2 else s["gate_scaled"], tile - 1)
                    in_chunk(pe, first, j, j, i)

        def down_pe(pe, first, steps, ready):
            for group in range(2):
                begin = first + steps * group

                def rhs(a, m):
                    return lambda row: a[:, bass.ds((m * 2 + row) * T, T)]

                def static(a, m):
                    return lambda row: a[:, (m * 2 + row) * T:(m * 2 + row + 1) * T]

                def chunk(m):
                    if group == 0:
                        ready(pe, m)
                    down_chunk(pe, begin, m, group, m == 0, m == steps - 1,
                               static(act_hi, m), static(act_lo, m))

                chunk(0)
                m = 1
                if steps > 8:
                    with pe.Fori(0, 2, 1) as i:
                        for j in range(4):
                            at = i * 4 + (1 + j)
                            if group == 0:
                                ready(pe, at)
                            down_chunk(pe, begin, 1 + j, group, False, False,
                                       rhs(act_hi, at), rhs(act_lo, at), i)
                    m = 9
                while m < steps:
                    chunk(m)
                    m += 1

        def ffn_pe(pe, f, n, first):
            ffn_up_pe(pe, f, n, first)
            pe.wait_ge(std_ready, n + 1)

            def ready(pe, m):
                pe.wait_ge(ffn_sems[f]["act_ready"], m * 2 + 2)
            down_pe(pe, first + FFN_UP, NF // 2, ready)

        def ple_pe(pe, layer, n, first):
            for j, what in enumerate(PLE_ORDER):
                k = int(what[1])
                if what[0] == "P":
                    if k == 0:
                        pe.wait_ge(p_ready, layer + 1)
                        pe.wait_ge(h_ready, tiles_before(n, KD - 1))
                    else:
                        pe.wait_ge(ple_term, KD * layer + GROUP)
                    slot = slot_of(first, j)
                    pe.wait_ge(split_ready, first + j + 1)
                    for d in range(GROUP):
                        for row in range(2):
                            b = row * GROUP + d
                            for part, (w, x) in enumerate(((w_hi, p_hi), (w_hi, p_lo), (w_lo, p_hi))):
                                last = pe.matmul(ps[:, 4 + d], w[:, slot, b], x[:, row],
                                                 start=(row == 0 and part == 0),
                                                 stop=(row == 1 and part == 2))
                    last.then_inc(chunk_used, 1)
                    continue
                if k == 3:
                    pe.wait_ge(std_ready, n + 1)
                if k >= GROUP:
                    pe.wait_ge(ple_scaled, KD * layer + k - GROUP + 1)
                in_chunk(pe, first, j, k % GROUP, n=n if k == 0 else None)
                if k == 0:
                    squares(pe, n)

        def z_pe(pe, n, first, tiles, extra=None):
            for j in range(tiles):
                if j >= 4:
                    pe.wait_ge(z_ready, z_base(n) + j - 3)
                in_chunk(pe, first, j, j % 4, n=n if j == 0 else None)
                if j == 0:
                    squares(pe, n)
                if extra:
                    extra(pe, j)

        def s5_tables_pe(pe):
            for part, ab in enumerate((ab_re, ab_im)):
                pe.wait_ge(tab, TAB["inputs"])
                if part == 0:
                    pe.wait_ge(z_ready, EV_IN)
                    pe.wait_ge(std_ready, 2)
                for j in range(S5_J):
                    last = pe.transpose(ps[:, 2 * part + j // 4, (j % 4) * P:(j % 4 + 1) * P],
                                        ab[:, j].rearrange("p q s -> p (q s)"), ident[:])
                    if j % 4 == 3:
                        last.then_inc(tab_pe, 1)
            for g in range(S5_G):
                j, rows = g // 2, slice(S5_N * (g % 2), S5_N * (g % 2) + S5_N)
                dst = ps[0:S5_P, 4 + 2 * (g % 2) + j // 4, (j % 4) * P:(j % 4 + 1) * P]
                first, rest = dst[:, 0:S5_P], dst[:, S5_P:]
                for part, (b, c0, c) in enumerate(((bb_re, c0_re, c_re), (bb_im, c0_im, c_im))):
                    pe.matmul(first, b[rows, j], c0[rows, j], start=(part == 0), stop=(part == 1))
                for part, (b, c0, c) in enumerate(((bb_re, c0_re, c_re), (bb_im, c0_im, c_im))):
                    last = pe.matmul(rest, b[rows, j],
                                     c[rows, j, :, 0:S5_L - 1].rearrange("p q s -> p s q"),
                                     start=(part == 0), stop=(part == 1))
            last.then_inc(tab_pe, 1)

        def ev_pe(pe):
            s5_tables_pe(pe)
            pe.wait_ge(u_moved, 32)
            pe.wait_ge(tab_act, 5)
            for part, w in enumerate((w_re, w_im)):
                for g in range(S5_G):
                    j, rows = g // 2, slice(S5_N * (g % 2), S5_N * (g % 2) + S5_N)
                    last = pe.matmul(ps[rows, 2 + part, j * S5_C:(j + 1) * S5_C], w[:, j, rows],
                                     u_grp[:, g], start=True, stop=True)
            last.then_inc(s5["x_done"], 1)
            pe.wait_ge(pads_ready, 6)
            pe.wait_ge(tab_taps, 1)
            for n in range(T // CH):
                last = pe.transpose(ps[:, 4 + n // 4, (n % 4) * P:(n % 4 + 1) * P],
                                    v_pad[:, n * CH:n * CH + P], ident[:])
            last.then_inc(ev["v_turned"], 1)

            def scores(m):
                if m:
                    pe.wait_ge(ev["exp"], HEADS * m)
                for kv in range(2):
                    rows = slice(HD * kv, HD * kv + HD)
                    for i in range(4):
                        for half in range(2):
                            n = 2 * m + half
                            dst = ps[HD * half:HD * half + HD, kv, i * P:(i + 1) * P]
                            last = pe.matmul(dst, zq[rows, i, n * CH:(n + 1) * CH],
                                             k_pad[rows, n * CH:n * CH + P], start=True, stop=n > 0)
                            if n == 0:
                                pe.matmul(dst, ones[0:1, 0:CH], neg_row[:], start=False, stop=True)
                last.then_inc(ev["scores"], 1)

            def turn(m):
                pe.wait_ge(ev["normed"], m + 1)
                if m:
                    pe.wait_ge(ev["turned_copied"], m)
                else:
                    pe.wait_ge(ev["v_ready"], 1)
                for hh in range(HEADS):
                    last = pe.transpose(ps[:, 4 + hh // 4, (hh % 4) * P:(hh % 4 + 1) * P],
                                        prob[:, m % 2, hh], ident[:])
                last.then_inc(ev["turned"], 1)

            def values(m):
                pe.wait_ge(ev["turned_copied"], m + 1)
                if m:
                    pe.wait_ge(ev["lo"], m)
                for half in range(2):
                    cols = slice(CH * half, CH * half + CH)
                    for kv in range(2):
                        rows = slice(HD * kv, HD * kv + HD)
                        last = pe.matmul(ps[rows, 6].rearrange("p (i q) -> p i q", i=4)[:, :, cols],
                                         v_band[:, 2 * m + half, rows],
                                         prob_t[:, m % 2, 4 * kv:4 * kv + 4, cols],
                                         start=True, stop=True)
                last.then_inc(ev["pv"], 1)

            scores(0)
            turn(0)
            scores(1)
            pe.wait_ge(s5["state_ready"], 2)
            pe.wait_ge(tab_zero, 2)
            for g in range(S5_G):
                j, rows = g // 2, slice(S5_N * (g % 2), S5_N * (g % 2) + S5_N)
                dst = ps[:, 2 + g % 2, j * S5_C:(j + 1) * S5_C]
                pe.matmul(dst, intra[:, S5_J * (g % 2) + j], u_grp[:, g], start=True, stop=False)
                pe.matmul(dst, c_re[rows, j].rearrange("p q s -> p (q s)"), s_re[rows, j, 0:S5_C],
                          start=False, stop=False)
                last = pe.matmul(dst, c_im[rows, j].rearrange("p q s -> p (q s)"),
                                 s_im[rows, j, 0:S5_C], start=False, stop=True)
            last.then_inc(s5["y_done"], 1)
            values(0)
            for m in range(1, NQ):
                turn(m)
                if m + 1 < NQ:
                    scores(m + 1)
                values(m)
            pe.wait_ge(tab_in, 80)
            pe.wait_ge(s5["gelu_done"], 1)
            pe.wait_ge(ev["exp"], HEADS * NQ)
            for t in range(S5_T):
                for k in range(S5_T):
                    last = pe.matmul(ps[:, t], w_glu[:, k, t * P:(t + 1) * P], y_act[:, k],
                                     start=(k == 0), stop=(k == S5_T - 1))
                last.then_inc(s5["glu_done"], 1)

        def od_norms_pe(pe, j):
            if j == 6:
                pe.wait_ge(od_s["sq_step"], 4)
                pe.matmul(ps[:, 5], ones[:], sm[0][:], start=True, stop=True).then_inc(od_s["ssq"], 1)
                pe.matmul(ps[:, 6], ones[:], sm[2][:], start=True, stop=True).then_inc(od_s["ssq"], 1)

        def od_pe(pe):
            pe.wait_ge(od_s["w_loaded"], 16 * 5)
            pe.wait_ge(od_s["latent"], 3)
            pe.wait_ge(z_ready, z_base(5) + OD_IN)
            pe.wait_ge(std_ready, 6)
            for number, (kind, i, bank) in enumerate(PREP):
                before = [x for x in range(number) if PREP[x][2] == bank]
                if before:
                    pe.wait_ge(od_s["prep_read"], before[-1] + 1)
                if kind == "q_idx" or kind == "q":
                    w = w_qidx if kind == "q_idx" else w_uq
                    for k in range(2):
                        last = pe.matmul(ps[:, bank], w[:, k, i * P:(i + 1) * P], cq[:, k],
                                         start=(k == 0), stop=(k == 1))
                elif kind == "weight":
                    rows = slice(HD, HD + IDX)
                    for m in range(NQ):
                        last = pe.transpose(ps[:, bank, m * IDX:(m + 1) * IDX],
                                            widx[rows, m * QB:(m + 1) * QB], ident[rows, rows])
                elif kind == "index":
                    m, head = divmod(i, IDX)
                    rows = slice(HD * (head % 2), HD * (head % 2) + HD)
                    pe.wait_ge(od_s["prep_read"], PREP.index(("q_idx", 1, 2)) + 1)
                    last = pe.matmul(ps[:, bank, 0:(m + 1) * QB],
                                     q_idx[rows, head // 2, m * QB:(m + 1) * QB],
                                     kidx[rows, 0:(m + 1) * QB], start=True, stop=True)
                elif kind == "k":
                    last = pe.matmul(ps[:, bank], w_uk[:, i * P:(i + 1) * P], ckv[:],
                                     start=True, stop=True)
                elif kind == "v":
                    last = pe.matmul(ps[:, bank], ckv[:, i * QB:(i + 1) * QB], w_uv[:],
                                     start=True, stop=True)
                else:
                    for head in range(4):
                        last = pe.transpose(ps[:, bank, head * P:(head + 1) * P],
                                            dv[:, head, i * QB:(i + 1) * QB], ident[:])
                last.then_inc(od_s["prep"], 1)

            def scores(u):
                kind, m, hh = UNITS[u]
                queries, keys = slice(m * QB, (m + 1) * QB), (m + 1) * QB
                for n, s in enumerate(JOBS_OF[u]):
                    if s >= 3:
                        pe.wait_ge(od_s["masked"], s - 2)
                    half = n if kind == "d" else hh % 2
                    rows = slice(HD * half, HD * half + HD)
                    if kind == "d":
                        lhs, rhs = dq[rows, hh, queries], dk[rows, hh, 0:keys]
                    else:
                        lhs, rhs = q_t[rows, hh // 2, queries], k_t[rows, hh // 2, 0:keys]
                    pe.matmul(ps[:, s % 3, 0:keys], lhs, rhs, start=True, stop=True)\
                      .then_inc(od_s["scores"], 1)

            def turn(u):
                kind, m, hh = UNITS[u]
                s = JOBS_OF[u][0]
                if kind == "d":
                    pe.wait_ge(od_s["normed"], u + 1)
                else:
                    pe.wait_ge(od_s["scaled"], u + 1)
                if u >= 2:
                    pe.wait_ge(od_s["turned_copied"], u - 1)
                for kb in range(m + 1):
                    last = pe.transpose(ps[:, 3 + u % 2, kb * QB:(kb + 1) * QB],
                                        sm[s % len(sm)][:, kb * QB:(kb + 1) * QB], ident[:])
                last.then_inc(od_s["turned"], 1)

            def values(u):
                kind, m, hh = UNITS[u]
                pe.wait_ge(od_s["turned_copied"], u + 1)
                if hh == 0:
                    if kind == "d" and m >= 2:
                        pe.wait_ge(od_s["d_copied"], m - 1)
                    if kind == "c" and m < 2:
                        pe.wait_ge(od_s["d_copied"], NQ - 1 + m)
                    if kind == "c" and m >= 2:
                        pe.wait_ge(od_s["c_lo"], m - 1)
                for kb in range(m + 1):
                    if kind == "d":
                        dst = ps[:, 5 + m % 2, hh * QB:(hh + 1) * QB]
                        lhs = v_d[:, kb, hh * P:(hh + 1) * P]
                    else:
                        rows = slice(HD * (hh % 2), HD * (hh % 2) + HD)
                        dst = ps[rows, 5 + m % 2, (hh // 2) * QB:(hh // 2 + 1) * QB]
                        lhs = v_h[:, kb, hh * HD:(hh + 1) * HD]
                    last = pe.matmul(dst, lhs, pt[:, u % 2, kb * QB:(kb + 1) * QB],
                                     start=(kb == 0), stop=(kb == m))
                last.then_inc(od_s["pv"], 1)

            pe.wait_ge(od_s["prep_read"], len(PREP))
            scores(0)
            scores(1)
            for u in range(len(UNITS)):
                if u + 2 < len(UNITS):
                    scores(u + 2)
                turn(u)
                if u:
                    values(u - 1)
                if u == NORM_AT:
                    pe.wait_ge(od_s["d_sq"], 1)
                    for i in range(4):
                        if i:
                            pe.wait_ge(od_s["d_sq"], i + 1)
                        pe.matmul(ps[:, 7], ones[:], sq_d[:, i], start=True, stop=True)\
                          .then_inc(od_s["d_ssq"], 1)
            values(len(UNITS) - 1)

        @block.tensor
        def _(pe):
            pe.wait_ge(const_ready, 4)
            ffn_pe(pe, 0, 0, STARTS[0])
            z_pe(pe, 1, STARTS[1], EV_IN)
            ev_pe(pe)

            def ev_ready(pe, m):
                if m == 0:
                    pe.wait_ge(ev["lo"], NQ)
                if m == 2:
                    pe.wait_ge(s5["lo_ready"], S5_T)
            down_pe(pe, STARTS[2], EV_OUT // 2, ev_ready)
            ffn_pe(pe, 1, 2, STARTS[3])
            ple_pe(pe, 0, 3, STARTS[4])
            ffn_pe(pe, 2, 4, STARTS[5])
            z_pe(pe, 5, STARTS[6], OD_IN, od_norms_pe)
            od_pe(pe)

            def od_ready(pe, m):
                if m == 0:
                    pe.wait_ge(od_s["c_lo"], NQ)
                if m == 2:
                    pe.wait_ge(od_s["d_lo"], 1)
            down_pe(pe, STARTS[7], OD_OUT // 2, od_ready)
            ffn_pe(pe, 3, 6, STARTS[8])
            ple_pe(pe, 1, 7, STARTS[9])
            pe.wait_ge(h_ready, tiles_before(8, KD - 1))
            squares(pe, 8)



def _out_tiles(np, w):
    k, m = w.shape
    return w.reshape(k // P, P, m // P, P).transpose(2, 1, 0, 3)


def _row_pairs(np, w):
    k, m = w.shape
    a = w.reshape(k // (2 * P), 2, P, m // (GROUP * P), GROUP, P).transpose(3, 0, 2, 1, 4, 5)
    return a.reshape(-1, P, BLOCKS, P)


def _heads(np, w, axis):
    order = [i + 4 * kv for i in range(4) for kv in range(2)]
    if axis:
        return w.reshape(w.shape[0], HEADS, HD)[:, order].reshape(w.shape[0], HEADS * HD)
    return w.reshape(HEADS, HD, w.shape[1])[order].reshape(HEADS * HD, w.shape[1])


def layout(np, x):
    g = {k: np.asarray(v) for k, v in x.items()}

    def ffn(i, j):
        gate, up = (_out_tiles(np, g[n][i, j]) for n in ("ffn_w_gate", "ffn_w_up"))
        both = np.stack([gate, up], 1).reshape(-1, P, BLOCKS, P)
        return [both, _row_pairs(np, g["ffn_w_down"][i, j])]

    def ple(i):
        gate = _out_tiles(np, g["ple_w_gate"][i])
        proj = _row_pairs(np, g["ple_w_proj"][i])
        return [np.stack([(gate if w[0] == "G" else proj)[int(w[1])] for w in PLE_ORDER])]

    ev = g["ev_w_in"][0]
    nq = HEADS * HD
    ev = np.concatenate([ev[:, nq + 256:], ev[:, nq:nq + 256], _heads(np, ev[:, :nq], 1)], 1)
    ev_out = g["ev_w_out"][0]
    ev_out = np.concatenate([_heads(np, ev_out[:nq], 0), ev_out[nq:]], 0)
    od = g["od_w_in"][0]
    od = np.concatenate([od[:, :452], np.zeros((D, 60), od.dtype), od[:, 452:]], 1)
    chunks = (ffn(0, 0) + [_out_tiles(np, ev), _row_pairs(np, ev_out)] + ffn(0, 1) + ple(0)
              + ffn(1, 0) + [_out_tiles(np, od), _row_pairs(np, g["od_w_out"][0])] + ffn(1, 1)
              + ple(1))
    weights = np.concatenate(chunks, 0)

    def states(a):
        rest = a.shape[2:]
        a = a.reshape((S5_J, 2 * S5_N) + rest)
        return np.ascontiguousarray(np.moveaxis(a, 0, 1))

    log_dt = np.broadcast_to(g["s5_log_dt"][0][:, None], (S5_G, S5_N))
    params = np.zeros((P, 16), np.float32)
    params[:, 0:2] = g["s5_d"][0].reshape(2, P).T
    params[:, 2:4] = g["c_q_norm"][0].reshape(2, P).T
    params[:, 4] = g["c_kv_norm"][0]
    params[:, 5] = g["d_head_norm"][0]
    lam = np.stack([g[n][0] for n in ("d_lam_q1", "d_lam_k1", "d_lam_q2", "d_lam_k2")])
    gains = np.concatenate([g["norms"].reshape(8, D), g["final_norm"][None]], 0)
    arrays = {
        "xT": g["x"][0].T, "pT": g["p"][:, 0].transpose(0, 2, 1), "weights": weights,
        "gains": gains.reshape(NORMS, KD, P).transpose(2, 0, 1),
        "s5_par": np.stack([states(g["s5_lam_re"][0]), states(g["s5_lam_im"][0]), states(log_dt)], 1),
        "s5_b_re": states(g["s5_b_re"][0]), "s5_b_im": states(g["s5_b_im"][0]),
        "s5_c_re": states(g["s5_c_re"][0].transpose(0, 2, 1)),
        "s5_c_im": states(g["s5_c_im"][0].transpose(0, 2, 1)),
        "w_glu": g["s5_w_glu"][0].reshape(2, P, 2 * P).transpose(1, 0, 2),
        "w_uq": g["c_w_uq"][0].reshape(2, P, 4 * P).transpose(1, 0, 2),
        "w_qidx": g["c_w_qidx"][0].reshape(2, P, 2 * P).transpose(1, 0, 2),
        "w_uk": g["c_w_uk"][0].reshape(P, 4 * P), "w_uv": g["c_w_uv"][0].reshape(P, 4 * P),
        "lam_vec": np.broadcast_to(lam, (P, 4, HD)),
        "sinks": np.broadcast_to(g["a_sinks"][0], (P, HEADS)),
        "params": params,
    }
    return {k: np.ascontiguousarray(v) for k, v in arrays.items()}


def kernel(**inputs):
    import numpy as np
    import concourse.bacc as bacc
    from concourse.bass_utils import run_bass_kernel_spmd

    nc = bacc.Bacc("TRN2", target_bir_lowering=False, num_devices=1)
    arrays = layout(np, inputs)
    A = {k: nc.dram_tensor("in_" + k, v.shape, mybir.dt.from_np(v.dtype), kind="ExternalInput").ap()
         for k, v in arrays.items()}
    out = nc.dram_tensor("out", (D, T), F32, kind="ExternalOutput").ap()
    encoder(nc, A, out)
    r = run_bass_kernel_spmd(nc, [{"in_" + k: v for k, v in arrays.items()}], core_ids=[0])
    return np.ascontiguousarray(r.results[0]["out"].T).reshape(1, T, D)
```

```python
from contextlib import ExitStack
import math

import concourse.bass as bass
from concourse import mybir

F32 = mybir.dt.float32
F32R = mybir.dt.float32r
I32 = mybir.dt.int32
ACT = mybir.ActivationFunctionType
ALU = mybir.AluOpType
AX_X = mybir.AxisListType.X
MULT, ADD, SUB = ALU.mult, ALU.add, ALU.subtract

P = 128
D = 1024
T = 512
FF = 2816
KD = D // P
NF = FF // P
BLOCKS = 8
SLOTS = 4
AHEAD = 2
EPS = 1e-6
GROUP = 4
QB = 128
NQ = T // QB
CH = 64
HD = 64
SCALE = HD ** -0.5
HEADS = 8
MASKED = -1e30
LOWEST = -3e38
KEEP = 128
PLE_K = 2
LAM_INIT = 0.8 - 0.6 * math.exp(-0.3)
NORMS = 9

S5_G, S5_P, S5_N = 16, 16, 64
S5_J = S5_G // 2
S5_L = 8
S5_C = T // S5_L
S5_T = 2

FFN_UP, FFN_DOWN = 2 * NF, NF
EV_IN, EV_OUT, OD_IN, OD_OUT = 8, 6, 16, 8
PLE_ORDER = ("P0", "G0", "G1", "G2", "G3", "G4", "P1", "G5", "G6", "G7")
LENGTHS = (FFN_UP + FFN_DOWN, EV_IN, EV_OUT, FFN_UP + FFN_DOWN, len(PLE_ORDER),
           FFN_UP + FFN_DOWN, OD_IN, OD_OUT, FFN_UP + FFN_DOWN, len(PLE_ORDER))
STARTS = tuple(sum(LENGTHS[:i]) for i in range(len(LENGTHS) + 1))
CHUNKS = STARTS[-1]

TWO_PI = (6.28125, 0.0019340515, 1.2556659e-06)
LN2 = (0.693359375, -2.12194440e-04)
ROUND = 1.5 * 2.0 ** 23


IDX = 4
CHOOSING = tuple(m for m in range(NQ) if (m + 1) * QB > KEEP)
ROUNDS = KEEP // 8
UNITS = tuple([("d", m, i) for m in range(NQ) for i in range(4)]
              + [("c", m, i) for m in range(NQ) for i in range(HEADS)])
UNIT_OF = tuple(u for u, (kind, _, _) in enumerate(UNITS) for _ in range(2 if kind == "d" else 1))
JOBS_OF = tuple(tuple(s for s, v in enumerate(UNIT_OF) if v == u) for u in range(len(UNITS)))
FIRST_ROUNDS = 12
NORM_AT = 30
PREP = tuple([("dv", i, 4 + i) for i in range(4)] + [("weight", 0, 0)]
             + [("q_idx", i, 1 + i) for i in range(2)]
             + [("index", m * IDX + i, 4 + i) for m in CHOOSING for i in range(IDX)]
             + [("q", i, i) for i in range(4)] + [("k", i, i) for i in range(4)]
             + [("v", i, 4 + i) for i in range(4)])


def encoder(nc, A, out):
    with ExitStack() as ctx:
        def sb(name, shape, dt=F32):
            where = nc.sbuf_base
            return ctx.enter_context(nc.sbuf_tensor(name, shape, dt)), where

        def sem(name):
            return ctx.enter_context(nc.semaphore(name))

        h, _ = sb("h", [P, KD, T])
        x_hi, at_x = sb("x_hi", [P, KD, T], F32R)
        x_lo, at_x_lo = sb("x_lo", [P, KD, T], F32R)
        act_hi, at_hi = sb("act_hi", [P, NF * T], F32R)
        act_lo, at_lo = sb("act_lo", [P, NF * T], F32R)
        raw, _ = sb("raw", [P, SLOTS, BLOCKS, P])
        w_hi, _ = sb("w_hi", [P, SLOTS, BLOCKS, P], F32R)
        w_lo, _ = sb("w_lo", [P, SLOTS, BLOCKS, P], F32R)
        t1, at_t1 = sb("t1", [P, 2, T])
        t2, at_t2 = sb("t2", [P, 2, T])
        square, at_square = sb("square", [P, 2, T])
        rstd, _ = sb("rstd", [P, T])
        std, at_std = sb("std", [P, T])
        sumsq, at_sumsq = sb("sumsq", [P, T])
        ident, _ = sb("ident", [P, P])
        ones, _ = sb("ones", [P, P])
        minus, _ = sb("minus", [P, 1])
        gains, _ = sb("gains", [P, NORMS, KD])
        eps, _ = sb("eps", [P, 1])
        s5_par, _ = sb("s5_par", [P, 3, S5_J])
        sc, _ = sb("sc", [P, 40, S5_J])
        stat, _ = sb("stat", [P, 8, 16])
        job, at_job = sb("job", [P, 4, 64])
        params, _ = sb("params", [P, 16])
        tile_bytes = T * 4

        def over(name, shape, where, dt=F32):
            return nc.alloc_sbuf_tensor_at(name, shape, dt, offset=where)

        free_hi, free_lo = at_hi + 8 * tile_bytes, at_lo + 8 * tile_bytes
        pads = CH + T

        zq = over("zq", [P, 4, T], free_hi)
        k_pad = over("k_pad", [P, pads], free_hi + 8192)
        v_pad = over("v_pad", [P, pads], free_hi + 8192 + 2304)
        v_band = over("v_band", [P, 8, P], free_hi + 12800)
        prob = over("prob", [P, 2, HEADS, P], at_x + 2048)
        s_re = over("s_re", [P, S5_J, S5_C + 1], free_hi + 25088)
        neg_row = over("neg_row", [1, P], free_hi + 25088 + 2080)
        sc_re = over("sc_re", [P, S5_J, S5_C], at_hi + 6 * tile_bytes)
        sc_im = over("sc_im", [P, S5_J, S5_C], at_hi + 7 * tile_bytes)
        u_ch = over("u_ch", [P, S5_T, T], free_lo)
        u_sc = over("u_sc", [P, S5_T, S5_L, S5_C], free_lo + 4096)
        u_grp = over("u_grp", [P, S5_G, S5_C], free_lo + 8192)
        prob_t = over("prob_t", [P, 2, HEADS, P], free_lo + 12288)
        y_grp = over("y_grp", [P, S5_G, S5_C], free_lo + 20480)
        y_ch = over("y_ch", [P, S5_T, S5_L * S5_C], free_lo + 24576)
        s_im = over("s_im", [P, S5_J, S5_C + 1], at_lo + 6 * tile_bytes)
        y_act = over("y_act", [P, S5_T, T], free_lo + 4096)
        glu = over("glu", [P, S5_T, T], free_lo + 20480)
        w_glu = over("w_glu", [P, 2, 2 * P], at_x)
        c_re = over("c_re", [P, S5_J, S5_P, S5_L], at_hi)
        c_im = over("c_im", [P, S5_J, S5_P, S5_L], at_hi + 4096)
        w_re = over("w_re", [P, S5_J, P], at_hi + 8192)
        w_im = over("w_im", [P, S5_J, P], at_lo)
        intra = over("intra", [P, S5_G, P], at_lo + 4096)
        e_re = over("e_re", [P, S5_J, S5_C], at_t1)
        e_im = over("e_im", [P, S5_J, S5_C], at_t1 + 2048)
        rot = [over(f"rot{i}", [P, S5_J, S5_C], a)
               for i, a in enumerate((at_t2, at_t2 + 2048, at_std, at_sumsq))]
        decay = over("decay", [P, S5_J, S5_C], at_square)

        b_re = over("b_re", [P, S5_J, S5_P], free_lo + 20480)
        b_im = over("b_im", [P, S5_J, S5_P], free_lo + 20992)
        bb_re = over("bb_re", [P, S5_J, S5_P], free_lo + 21504)
        bb_im = over("bb_im", [P, S5_J, S5_P], free_lo + 22016)
        c0_re = over("c0_re", [P, S5_J, S5_P], free_lo + 22528)
        c0_im = over("c0_im", [P, S5_J, S5_P], free_lo + 23040)
        m_a = over("m_a", [P, 256], at_t2)
        m_b = over("m_b", [P, 256], at_t2 + 1024)
        m_c = over("m_c", [P, P], free_hi + 12800)
        m_d = over("m_d", [P, P], free_hi + 13312)
        pw_re = over("pw_re", [P, S5_L + 1, S5_J], at_job)
        pw_im = over("pw_im", [P, S5_L + 1, S5_J], at_job + 288)
        expo = over("expo", [P, 3 * S5_J], at_job + 576, I32)
        ab_re = over("ab_re", [P, S5_J, S5_P, S5_L], free_hi + 16896)
        ab_im = over("ab_im", [P, S5_J, S5_P, S5_L], free_hi + 20992)
        placed = over("placed", [P, S5_G, S5_L, S5_P], free_hi + 16896)
        taps = over("taps", [S5_P, S5_G, S5_L * S5_P], free_lo + 12288)

        dq = over("dq", [P, 4, T], free_hi)
        dk = over("dk", [P, 4, T], free_hi + 8192)
        cq = over("cq", [P, 2, T], free_hi + 16384)
        ckv = over("ckv", [P, T], free_hi + 20480)
        kidx = over("kidx", [P, T], free_hi + 22528)
        causal = over("causal", [P, T], free_hi + 24576)
        dv = over("dv", [P, 4, T], free_lo)
        kept = [over(f"kept{m}", [P, (m + 1) * QB], a)
                for m, a in zip(CHOOSING, (free_lo + 2048, free_lo + 22528, free_lo))]
        pt = over("pt", [P, 2, T], free_lo + 4096)
        w_uq = over("w_uq", [P, 2, 4 * P], free_lo + 8192)
        w_qidx = over("w_qidx", [P, 2, 2 * P], free_lo + 12288)
        w_uk = over("w_uk", [P, 4 * P], free_lo + 14336)
        w_uv = over("w_uv", [P, 4 * P], free_lo + 16384)
        q_idx = over("q_idx", [P, 2, T], free_lo + 18432)
        work = over("work", [P, T], free_lo + 24576)
        widx = over("widx", [P, T], free_lo + 26624)
        q_t = over("q_t", [P, 4, T], at_x)
        k_t = over("k_t", [P, 4, T], at_x + 8192)
        v_h = over("v_h", [P, 4, T], at_x_lo)
        v_d = over("v_d", [P, 4, T], at_x_lo + 8192)
        sm = [over(f"sm{i}", [P, T], a) for i, a in enumerate(
            (at_t1, at_t1 + 2048, at_t2, at_t2 + 2048, at_square, at_square + 2048))]
        od = over("od", [P, 4, T], free_lo + 8192)
        sq_d = over("sq_d", [P, 4, T], free_hi)
        lam_vec = over("lam_vec", [P, 4, HD], free_hi + 26624)
        lam_prod = over("lam_prod", [P, 2, HD], free_hi + 27648)

        p_raw = over("p_raw", [P, PLE_K, T], at_hi)
        p_hi = over("p_hi", [P, PLE_K, T], at_hi + 2 * tile_bytes, F32R)
        p_lo = over("p_lo", [P, PLE_K, T], at_hi + 4 * tile_bytes, F32R)
        result = over("result", [P, KD, T], free_lo)

        ps = ctx.enter_context(nc.psum_tensor("ps", [P, 8, T], F32))
        scratch_u = nc.dram_tensor("scratch_u", [S5_G * S5_P, S5_L, S5_C], F32).ap()
        scratch_y = nc.dram_tensor("scratch_y", [S5_G * S5_P, S5_L, S5_C], F32).ap()

        raw_loaded = [sem(f"raw_loaded{i}") for i in range(SLOTS)]
        hi_ready = sem("hi_ready")
        split_ready = sem("split_ready")
        chunk_used = sem("chunk_used")
        h_loaded = [sem(f"h_loaded{i}") for i in range(KD // 2)]
        s5_loaded = sem("s5_loaded")
        gains_loaded = sem("gains_loaded")
        param_loaded = sem("param_loaded")
        const_ready = sem("const_ready")
        h_ready = sem("h_ready")
        x_hi_ready = sem("x_hi_ready")
        x_lo_ready = sem("x_lo_ready")
        sum_step = sem("sum_step")
        ssq_ready = sem("ssq_ready")
        std_ready = sem("std_ready")
        rstd_ready = sem("rstd_ready")
        tile_done = sem("tile_done")
        z_ready = sem("z_ready")
        p_loaded = sem("p_loaded")
        p_hi_ready = sem("p_hi_ready")
        p_ready = sem("p_ready")
        ple_scaled = sem("ple_scaled")
        ple_gate = sem("ple_gate")
        ple_term = sem("ple_term")
        stored = sem("stored")
        out_ready = sem("out_ready")
        ffn_sems = [{n: sem(f"ffn{i}_{n}") for n in (
            "gate_scaled", "silu_done", "up_scaled", "prod_done", "act_hi_ready", "act_ready")}
            for i in range(4)]
        tab = sem("tab")
        tab_act = sem("tab_act")
        tab_pe = sem("tab_pe")
        tab_taps = sem("tab_taps")
        tab_zero = sem("tab_zero")
        tab_c = sem("tab_c")
        tab_moved = sem("tab_moved")
        tab_in = sem("tab_in")
        pads_ready = sem("pads_ready")
        u_moved = sem("u_moved")
        u_sorted = sem("u_sorted")
        y_moved = sem("y_moved")
        s5 = {n: sem(f"s5_{n}") for n in ("x_done", "step", "state_ready", "y_done", "y_copied",
                                          "skip_done", "gelu_done", "glu_done", "gate_ready",
                                          "prod_done", "hi_ready", "lo_ready")}
        ev = {n: sem(f"ev_{n}") for n in ("v_turned", "v_ready", "scores", "max", "bias", "exp",
                                          "sink_exp", "recip", "normed", "turned",
                                          "turned_copied", "pv", "hi", "lo")}
        od_s = {n: sem(f"od_{n}") for n in (
            "w_loaded", "sq_step", "ssq", "std", "rstd", "latent", "prep", "prep_read", "lam",
            "index_step", "sel_step", "const", "scores", "masked", "bias", "exp",
            "recip", "scaled", "normed", "turned", "turned_copied", "pv", "c_hi", "c_lo", "d_copied",
            "d_sq", "d_ssq", "d_std", "d_rstd", "d_diag", "d_spread", "d_out", "d_hi", "d_lo")}

        block = ctx.enter_context(nc.Block())

        def slot_of(first, j):
            return (first + j) % SLOTS

        def turn_of(first, j, i=0):
            return i + (first + j) // SLOTS

        def split_hi(act, first, j, i=0):
            if isinstance(i, int) and first + 4 * i + j >= CHUNKS:
                return
            slot = slot_of(first, j)
            act.wait_ge(raw_loaded[slot], turn_of(first, j, i) * 16 + 16)
            if not isinstance(i, int) or first + 4 * i + j >= SLOTS:
                act.wait_ge(chunk_used, i * 4 + (first + j - SLOTS + 1))
            act.activation(w_hi[:, slot], raw[:, slot], ACT.Copy).then_inc(hi_ready, 1)

        def split_lo(dve, first, j, i=0):
            if isinstance(i, int) and first + 4 * i + j >= CHUNKS:
                return
            slot = slot_of(first, j)
            dve.wait_ge(hi_ready, i * 4 + (first + j + 1))
            dve.tensor_tensor(w_lo[:, slot], raw[:, slot], w_hi[:, slot].bitcast(F32), SUB)\
               .then_inc(split_ready, 1)

        def z_base(n):
            return 0 if n == 1 else EV_IN

        def tiles_before(n, k):
            return KD * (n - 1) + k + 1

        AFTER = 8

        SUM_STEPS = 2 * KD - 1

        def gained_lo(dve, n, k):
            dve.wait_ge(x_hi_ready, KD * n + k + 1)
            if n == 0:
                dve.wait_ge(h_loaded[k // 2], 16)
            dve.scalar_tensor_tensor(out=x_lo[:, k], in0=h[:, k], scalar=gains[:, n, k:k + 1],
                                     in1=x_hi[:, k].bitcast(F32), op0=MULT, op1=SUB)\
               .then_inc(x_lo_ready, 1)

        def reciprocal_root(dve, n):
            dve.wait_ge(std_ready, n + 1)
            dve.reciprocal(rstd[:], std[:]).then_inc(rstd_ready, 1)
            dve.wait_ge(rstd_ready, n + 1)

        def ffn_up_dve(dve, f, n, first):
            s = ffn_sems[f]

            def gate(i, b):
                dve.wait_ge(chunk_used, i * 4 + (first + 2 * b + 1))
                dve.tensor_tensor(t1[:, b], ps[:, 2 * b], rstd[:], MULT).then_inc(s["gate_scaled"], 1)

            def up(i, b):
                dve.wait_ge(chunk_used, i * 4 + (first + 2 * b + 2))
                dve.tensor_tensor(t2[:, b], ps[:, 2 * b + 1], rstd[:], MULT)\
                   .then_inc(s["up_scaled"], 1)
                dve.wait_ge(s["up_scaled"], i * 2 + (b + 1))
                dve.wait_ge(s["silu_done"], i * 2 + (b + 1))
                dve.tensor_tensor(t2[:, b], t2[:, b], t1[:, b], MULT).then_inc(s["prod_done"], 1)

            def low(i, b):
                dve.wait_ge(s["act_hi_ready"], i * 2 + (b + 1))
                span = bass.ds((i * 2 + b) * T, T)
                dve.tensor_tensor(act_lo[:, span], t2[:, b], act_hi[:, span].bitcast(F32), SUB)\
                   .then_inc(s["act_ready"], 1)

            def two_tiles(i, peeled=False):
                split_lo(dve, first, AHEAD, i)
                split_lo(dve, first, AHEAD + 1, i)
                if peeled:
                    reciprocal_root(dve, n)
                gate(i, 0)
                split_lo(dve, first, AHEAD + 2, i)
                up(i, 0)
                split_lo(dve, first, AHEAD + 3, i)
                gate(i, 1)
                low(i, 0)
                up(i, 1)
                low(i, 1)

            two_tiles(0, peeled=True)
            with dve.Fori(1, NF // 2, 1) as i:
                two_tiles(i)

        def down_dve(dve, n, first, steps, q, scale, after=None, beside=()):
            def update(k):
                group, d = divmod(k, GROUP)
                if d < GROUP - 1:
                    dve.wait_ge(tile_done, 3 * (2 * q + group) + d + 1)
                else:
                    dve.wait_ge(chunk_used, first + steps * (group + 1))
                dve.scalar_tensor_tensor(out=h[:, k], in0=ps[:, (4, 0)[group] + d], scalar=scale,
                                         in1=h[:, k], op0=MULT, op1=ADD).then_inc(h_ready, 1)

            def low(k):
                if n < NORMS - 1:
                    gained_lo(dve, n, k)

            loops = steps // 4
            if loops > 1:
                with dve.Fori(0, loops, 1) as i:
                    for j in range(4):
                        split_lo(dve, first, AHEAD + j, i)
            else:
                loops = 0
            for j in range(4 * loops, steps):
                split_lo(dve, first, AHEAD + j)
            for j in range(steps):
                split_lo(dve, first, AHEAD + steps + j)
                if j < GROUP:
                    update(j)
                    if j:
                        low(j - 1)
                elif j - GROUP < len(beside):
                    beside[j - GROUP](dve)
                if after and j == AFTER:
                    after(dve)
            for k in range(min(steps, GROUP), KD):
                update(k)
                low(k - 1)
            low(KD - 1)

        def embedding_lo(dve, layer):
            dve.wait_ge(p_hi_ready, layer + 1)
            dve.tensor_tensor(p_lo[:], p_raw[:], p_hi[:].bitcast(F32), SUB).then_inc(p_ready, 1)

        def ple_dve(dve, layer, n, first):

            def finish(k):
                dve.wait_ge(ple_gate, KD * layer + k + 1)
                dve.tensor_tensor(t2[:, k % 2], ps[:, 4 + k % GROUP], t1[:, k % 2], MULT)\
                   .then_inc(ple_term, 1)
                dve.wait_ge(ple_term, KD * layer + k + 1)
                dve.tensor_tensor(h[:, k], h[:, k], t2[:, k % 2], ADD).then_inc(h_ready, 1)

            for j, what in enumerate(PLE_ORDER):
                if what != "G1":
                    split_lo(dve, first, AHEAD + j)
                if what[0] == "G":
                    k = int(what[1])
                    if k == 0:
                        split_lo(dve, first, AHEAD + j + 1)
                        reciprocal_root(dve, n)
                    dve.wait_ge(chunk_used, first + j + 1)
                    if k >= GROUP:
                        dve.wait_ge(chunk_used, first + PLE_ORDER.index("P1") + 1)
                    dve.tensor_tensor(t1[:, k % 2], ps[:, k % GROUP], rstd[:], MULT)\
                       .then_inc(ple_scaled, 1)
                    if k == KD - 1 and n + 1 < NORMS - 1:
                        gained_lo(dve, n + 1, 0)
                    finish(k)
            if n + 1 < NORMS - 1:
                for k in range(1, KD):
                    gained_lo(dve, n + 1, k)

        def scale_tile(dve, n, first, j, bank, dsts):
            dve.wait_ge(chunk_used, first + j + 1)
            for dst, rows in dsts:
                last = dve.tensor_tensor(dst, ps[rows, bank], rstd[rows], MULT)
            last.then_inc(z_ready, 1)

        def ev_in_dve(dve, n, first):
            everything = slice(0, P)
            dsts = [u_ch[:, 0], u_ch[:, 1], k_pad[:, CH:], v_pad[:, CH:]] + [zq[:, i] for i in range(4)]
            for j in range(EV_IN):
                if j != 1:
                    split_lo(dve, first, AHEAD + j)
                if j == 0:
                    split_lo(dve, first, AHEAD + 1)
                    reciprocal_root(dve, n)
                scale_tile(dve, n, first, j, j % 4, [(dsts[j], everything)])
                if j == 0:
                    s5_inputs_dve(dve)
                    s5_decay_dve(dve)
                elif j <= 4:
                    for part in range(2):
                        s5_step_dve(dve, 2 * (j - 1) + part)

        DT, LRDT, LRDT8, TH, TH8, K_, RES, ACC, MAG, MAG8 = 0, 1, 2, 3, 4, 5, 7, 9, 11, 12
        SIN, SIN8, COS, COS8 = 16, 17, 18, 19
        AR, AI, UR, UI, DEN, ZR, ZI, TA, TB = range(20, 29)
        SINKS = 36
        LAM = 30

        TAB = {}

        def row(r, n=1):
            return sc[:, r:r + n]

        FULL = [P, S5_J, S5_P]
        count = [0]

        def tab_do(dve, ins):
            count[0] += 1
            ins.then_inc(tab, 1)
            dve.wait_ge(tab, count[0])

        def cmul(do, temps, o_re, o_im, a_re, a_im, b_re_, b_im_, shape, sign=1):
            n = 1
            for x in shape[1:]:
                n *= x
            dims = " ".join("abc"[:len(shape) - 1])
            sizes = {c: v for c, v in zip("abc", shape[1:])}
            a, b = (t[:, 0:n].rearrange(f"p ({dims}) -> p {dims}", **sizes) for t in temps)
            do(a, a_re, b_re_, MULT)
            do(b, a_im, b_im_, MULT)
            do(o_re, a, b, SUB)
            do(a, a_re, b_im_, MULT)
            do(b, a_im, b_re_, MULT)
            if sign < 0:
                do(a, a, b, ADD)
                do(o_im, a, minus[:, 0:1].unsqueeze(2).to_broadcast(shape), MULT)
            else:
                do(o_im, a, b, ADD)

        def dve_cmul(dve, *args):
            cmul(lambda o, a, b, op: tab_do(dve, dve.tensor_tensor(o, a, b, op)), (m_a, m_b), *args)

        def s5_exp(do, dve, dst, src, n):
            k, r, a = row(K_, n), row(RES, n), row(ACC, n)
            do(dve.tensor_scalar(k, src, 1.0 / math.log(2.0), ROUND, MULT, ADD))
            do(dve.tensor_scalar(k, k, ROUND, None, SUB))
            do(dve.tensor_scalar(k, k, -126.0, 127.0, ALU.max, ALU.min))
            do(dve.scalar_tensor_tensor(out=r, in0=k, scalar=-LN2[0], in1=src, op0=MULT, op1=ADD))
            do(dve.scalar_tensor_tensor(out=r, in0=k, scalar=-LN2[1], in1=r, op0=MULT, op1=ADD))
            do(dve.tensor_scalar(a, r, 1.0 / 5040, 1.0 / 720, MULT, ADD))
            for c in (1.0 / 120, 1.0 / 24, 1.0 / 6, 0.5, 1.0, 1.0):
                do(dve.tensor_tensor(a, a, r, MULT))
                do(dve.tensor_scalar(a, a, c, None, ADD))
            whole = expo[:, 0:n * S5_J].rearrange("p (a j) -> p a j", a=n)
            do(dve.tensor_scalar(whole, k, 127.0, 2.0 ** 23, ADD, MULT))
            do(dve.tensor_tensor(dst, a, whole.bitcast(F32), MULT))

        def s5_angles_dve(dve):
            def do(ins):
                tab_do(dve, ins)

            lr, li, ldt = (s5_par[:, i:i + 1] for i in range(3))
            s5_exp(do, dve, row(DT), ldt, 1)
            do(dve.tensor_tensor(row(LRDT), lr, row(DT), MULT))
            do(dve.tensor_scalar(row(LRDT8), row(LRDT), float(S5_L), None, MULT))
            do(dve.tensor_tensor(row(TH), li, row(DT), MULT))
            do(dve.tensor_scalar(row(TH8), row(TH), float(S5_L), None, MULT))
            k, r = row(12, 2), row(14, 2)
            do(dve.tensor_scalar(k, row(TH, 2), 1.0 / (2 * math.pi), ROUND, MULT, ADD))
            do(dve.tensor_scalar(k, k, ROUND, None, SUB))
            do(dve.scalar_tensor_tensor(out=r, in0=k, scalar=-TWO_PI[0], in1=row(TH, 2), op0=MULT, op1=ADD))
            do(dve.scalar_tensor_tensor(out=r, in0=k, scalar=-TWO_PI[1], in1=r, op0=MULT, op1=ADD))
            do(dve.scalar_tensor_tensor(out=r, in0=k, scalar=-TWO_PI[2], in1=r, op0=MULT, op1=ADD))
            do(dve.tensor_scalar(row(SIN, 2), r, 3.1415925, -3.1415925, ALU.min, ALU.max))
            do(dve.tensor_scalar(r, r, math.pi / 2, None, ADD))
            do(dve.tensor_scalar(k, r, math.pi, -2 * math.pi, ALU.is_gt, MULT))
            do(dve.tensor_tensor(r, r, k, ADD))
            do(dve.tensor_scalar(row(COS, 2), r, 3.1415925, -3.1415925, ALU.min, ALU.max))
            TAB["angles"] = count[0]

        def s5_zero_order_dve(dve):
            def do(ins):
                tab_do(dve, ins)

            lr, li = (s5_par[:, i:i + 1] for i in range(2))
            s5_exp(do, dve, row(MAG, 2), row(LRDT, 2), 2)
            dve.wait_ge(tab_act, 1)
            do(dve.tensor_tensor(row(AR), row(MAG), row(COS), MULT))
            do(dve.tensor_tensor(row(AI), row(MAG), row(SIN), MULT))
            do(dve.tensor_tensor(row(TA), lr, lr, MULT))
            do(dve.tensor_tensor(row(TB), li, li, MULT))
            do(dve.tensor_tensor(row(TA), row(TA), row(TB), ADD))
            do(dve.reciprocal(row(DEN), row(TA)))
            do(dve.tensor_scalar(row(UR), row(AR), -1.0, None, ADD))
            do(dve.tensor_tensor(row(TA), row(UR), lr, MULT))
            do(dve.tensor_tensor(row(TB), row(AI), li, MULT))
            do(dve.tensor_tensor(row(TA), row(TA), row(TB), ADD))
            do(dve.tensor_tensor(row(ZR), row(TA), row(DEN), MULT))
            do(dve.tensor_tensor(row(TA), row(AI), lr, MULT))
            do(dve.tensor_tensor(row(TB), row(UR), li, MULT))
            do(dve.tensor_tensor(row(TA), row(TA), row(TB), SUB))
            do(dve.tensor_tensor(row(ZI), row(TA), row(DEN), MULT))

        def s5_powers_dve(dve):
            tab_do(dve, dve.memset(pw_re[:, 0], 1.0))
            tab_do(dve, dve.memset(pw_im[:, 0], 0.0))
            tab_do(dve, dve.tensor_copy(pw_re[:, 1:2], row(AR)))
            tab_do(dve, dve.tensor_copy(pw_im[:, 1:2], row(AI)))
            n = 1
            while n < S5_L:
                dve_cmul(dve, pw_re[:, n + 1:2 * n + 1], pw_im[:, n + 1:2 * n + 1],
                         pw_re[:, 1:n + 1], pw_im[:, 1:n + 1],
                         pw_re[:, n:n + 1].to_broadcast([P, n, S5_J]),
                         pw_im[:, n:n + 1].to_broadcast([P, n, S5_J]), [P, n, S5_J])
                n *= 2
            TAB["powers"] = count[0]

        def power(s):
            return [pw[:, s].unsqueeze(2).to_broadcast(FULL) for pw in (pw_re, pw_im)]

        def s5_inputs_dve(dve):
            dve.wait_ge(tab_in, 64)
            z = [sc[:, r].unsqueeze(2).to_broadcast(FULL) for r in (ZR, ZI)]
            dve_cmul(dve, bb_re[:], bb_im[:], b_re[:], b_im[:], *z, FULL)

        def s5_step_dve(dve, s):
            dve_cmul(dve, ab_re[:, :, :, s], ab_im[:, :, :, s], bb_re[:], bb_im[:],
                     *power(S5_L - 1 - s), FULL)
            TAB["inputs"] = count[0]

        def s5_rotor_start_dve(dve):
            tab_do(dve, dve.memset(e_re[:, :, 0], 1.0))
            tab_do(dve, dve.memset(e_im[:, :, 0], 0.0))
            tab_do(dve, dve.tensor_copy(row(UR), row(COS8)))
            tab_do(dve, dve.tensor_copy(row(UI), row(SIN8)))

        def s5_rotor_dve(dve, n):
            def do(ins):
                tab_do(dve, ins)

            size = [P, S5_J, n]
            dve_cmul(dve, e_re[:, :, n:2 * n], e_im[:, :, n:2 * n], e_re[:, :, 0:n],
                     e_im[:, :, 0:n], sc[:, UR].unsqueeze(2).to_broadcast(size),
                     sc[:, UI].unsqueeze(2).to_broadcast(size), size)
            if 2 * n < S5_C:
                dve_cmul(dve, row(TA), row(TB), row(UR), row(UI), row(UR), row(UI), [P, 1, S5_J])
                do(dve.tensor_copy(row(UR), row(TA)))
                do(dve.tensor_copy(row(UI), row(TB)))

        def s5_decay_dve(dve):
            tab_do(dve, dve.tensor_copy(decay[:], sc[:, MAG8].unsqueeze(2)
                                        .to_broadcast([P, S5_J, S5_C])))
            tab_do(dve, dve.memset(decay[:, :, 0], 0.0))

        S5_BESIDE = (s5_zero_order_dve, s5_powers_dve, s5_rotor_start_dve,
                     lambda dve: (s5_rotor_dve(dve, 1), s5_rotor_dve(dve, 2)),
                     lambda dve: (s5_rotor_dve(dve, 4), s5_rotor_dve(dve, 8)),
                     lambda dve: s5_rotor_dve(dve, 16), lambda dve: s5_rotor_dve(dve, 32))

        def ev_dve(dve):
            steps = [0]

            def do(ins):
                steps[0] += 1
                ins.then_inc(s5["step"], 1)
                dve.wait_ge(s5["step"], steps[0])

            def biggest(m):
                dve.wait_ge(ev["scores"], m + 1)
                dve.tensor_reduce(stat[:, 0 + m % 2, 8:16],
                                  ps[:, 2 * (m % 2):2 * (m % 2) + 2]
                                  .rearrange("p b (h k) -> p (b h) k", h=4), AX_X, ALU.max)\
                   .then_inc(ev["max"], 1)
                dve.wait_ge(ev["max"], m + 1)
                do(dve.scalar_tensor_tensor(out=stat[:, m % 2, 0:HEADS], in0=stat[:, m % 2, 8:16],
                                            scalar=-SCALE, in1=sc[:, SINKS + 1], op0=MULT, op1=ALU.min))
                dve.tensor_tensor(stat[:, 6 + m % 2, 0:HEADS], stat[:, m % 2, 0:HEADS], sc[:, SINKS],
                                  ADD).then_inc(ev["bias"], 1)

            def recip(m):
                dve.wait_ge(ev["sink_exp"], m + 1)
                dve.wait_ge(ev["exp"], HEADS * (m + 1))
                do(dve.tensor_tensor(stat[:, 2 + m % 2, 8:16], stat[:, 2 + m % 2, 0:HEADS],
                                     stat[:, 6 + m % 2, 0:HEADS], ADD))
                dve.reciprocal(stat[:, 4 + m % 2, 0:HEADS], stat[:, 2 + m % 2, 8:16])\
                   .then_inc(ev["recip"], 1)

            def out_lo(m):
                dve.wait_ge(ev["hi"], m + 1)
                span = [a[:, 0:4 * T].rearrange("p (i t) -> p i t", i=4)[:, :, m * QB:(m + 1) * QB]
                        for a in (act_hi, act_lo)]
                dve.tensor_tensor(span[1], ps[:, 6].rearrange("p (i q) -> p i q", i=4),
                                  span[0].bitcast(F32), SUB).then_inc(ev["lo"], 1)

            dve.wait_ge(param_loaded, 32)
            do(dve.tensor_scalar(sc[:, SINKS + 1], sc[:, SINKS], -1.0, None, MULT))
            biggest(0)
            dve.wait_ge(s5["x_done"], 1)
            v_re = ps[:, 2].rearrange("p (j c) -> p j c", j=S5_J)
            v_im = ps[:, 3].rearrange("p (j c) -> p j c", j=S5_J)
            do(dve.tensor_tensor(rot[0][:], v_re, e_re[:], MULT))
            do(dve.tensor_tensor(rot[1][:], v_im, e_im[:], MULT))
            do(dve.tensor_tensor(rot[2][:], v_im, e_re[:], MULT))
            do(dve.tensor_tensor(rot[3][:], v_re, e_im[:], MULT))
            TAB["x_read"] = steps[0]
            do(dve.tensor_tensor(rot[0][:], rot[0][:], rot[1][:], ADD))
            do(dve.tensor_tensor(rot[2][:], rot[2][:], rot[3][:], SUB))

            recip(0)
            flat = "p j c -> p (j c)"
            do(dve.tensor_tensor_scan(sc_re[:].rearrange(flat), decay[:].rearrange(flat),
                                      rot[0][:].rearrange(flat), 0.0, MULT, ADD))
            do(dve.tensor_tensor_scan(sc_im[:].rearrange(flat), decay[:].rearrange(flat),
                                      rot[2][:].rearrange(flat), 0.0, MULT, ADD))
            do(dve.tensor_tensor(rot[0][:], sc_re[:], e_re[:], MULT))
            do(dve.tensor_tensor(rot[1][:], sc_im[:], e_im[:], MULT))
            do(dve.tensor_tensor(rot[2][:], sc_re[:], e_im[:], MULT))
            do(dve.tensor_tensor(rot[3][:], sc_im[:], e_re[:], MULT))
            dve.wait_ge(pads_ready, 6)
            dve.tensor_tensor(s_re[:, :, 1:], rot[0][:], rot[1][:], SUB).then_inc(s5["state_ready"], 1)
            dve.tensor_tensor(s_im[:, :, 1:], rot[2][:], rot[3][:], ADD).then_inc(s5["state_ready"], 1)
            biggest(1)
            dve.wait_ge(tab_moved, 16 * S5_L)
            dve.tensor_copy(intra[:].rearrange("p g (q s) -> p g q s", s=S5_L),
                            placed[:].rearrange("p g s q -> p g q s")).then_inc(tab_zero, 1)
            recip(1)
            for m in range(NQ):
                if m + 2 < NQ:
                    biggest(m + 2)
                    recip(m + 2)
                out_lo(m)
            dve.wait_ge(y_moved, 48)
            for t in range(S5_T):
                dve.scalar_tensor_tensor(
                    out=y_act[:, t].rearrange("p (c s) -> p c s", s=S5_L),
                    in0=u_ch[:, t].rearrange("p (c s) -> p c s", s=S5_L),
                    scalar=params[:, t:t + 1],
                    in1=y_ch[:, t].rearrange("p (s c) -> p c s", s=S5_L),
                    op0=MULT, op1=ADD).then_inc(s5["skip_done"], 1)
            for t in range(S5_T):
                dve.wait_ge(s5["gate_ready"], t + 1)
                dve.tensor_tensor(glu[:, t], glu[:, t], y_act[:, t], MULT).then_inc(s5["prod_done"], 1)
            for t in range(S5_T):
                dve.wait_ge(s5["hi_ready"], t + 1)
                span = slice((4 + t) * T, (5 + t) * T)
                dve.tensor_tensor(act_lo[:, span], glu[:, t], act_hi[:, span].bitcast(F32), SUB)\
                   .then_inc(s5["lo_ready"], 1)

        def od_in_dve(dve, n, first):
            half, whole = slice(0, HD), slice(0, P)
            for j in range(OD_IN):
                if j != 1:
                    split_lo(dve, first, AHEAD + j)
                if j == 0:
                    split_lo(dve, first, AHEAD + 1)
                    reciprocal_root(dve, n)
                if j < 2:
                    dsts = [(cq[:, j], whole)]
                elif j == 2:
                    dsts = [(ckv[:], whole)]
                elif j == 3:
                    rows = slice(HD, HD + IDX)
                    dsts = [(kidx[0:HD], half), (kidx[HD:P], half), (widx[rows], rows)]
                else:
                    dsts = [((dq, dk, dv)[j // 4 - 1][:, j % 4], whole)]
                scale_tile(dve, n, first, j, j % 4, dsts)
                if j == 8:
                    dve.wait_ge(od_s["std"], 2)
                    for i in range(2):
                        dve.reciprocal(sm[3 + i][:], sm[3 + i][:]).then_inc(od_s["rstd"], 1)
                    dve.wait_ge(od_s["rstd"], 2)
                    for i, x in enumerate((cq[:, 0], cq[:, 1], ckv[:])):
                        dve.scalar_tensor_tensor(out=x, in0=x, scalar=params[:, 2 + i:3 + i],
                                                 in1=sm[3 + i // 2][:], op0=MULT, op1=MULT)\
                           .then_inc(od_s["latent"], 1)

        def od_dve(dve):
            od_in_dve(dve, 5, STARTS[6])
            dve.wait_ge(od_s["w_loaded"], 16 * 5)
            dve.tensor_tensor(lam_prod[:], lam_vec[:, 0:4:2], lam_vec[:, 1:4:2], MULT)\
               .then_inc(od_s["lam"], 1)
            dve.wait_ge(od_s["lam"], 1)
            dve.tensor_reduce(sc[:, LAM, 0:2], lam_prod[:], AX_X, ADD).then_inc(od_s["lam"], 1)
            dve.wait_ge(od_s["lam"], 3)
            dve.scalar_tensor_tensor(out=sc[:, LAM, 2:3], in0=sc[:, LAM, 1:2], scalar=-LAM_INIT,
                                     in1=sc[:, LAM, 0:1], op0=ADD, op1=SUB).then_inc(od_s["lam"], 1)
            dve.tensor_scalar(sc[:, LAM, 3:4], params[:, 5:6], 1.0 - LAM_INIT, None, MULT)\
               .then_inc(od_s["lam"], 1)
            dve.wait_ge(od_s["lam"], 5)

            step = 0
            for b, m in enumerate(CHOOSING):
                keys = (m + 1) * QB
                for i in range(IDX):
                    dve.wait_ge(od_s["prep_read"], PREP.index(("index", m * IDX + i, 4 + i)) + 1)
                    if i:
                        dve.wait_ge(od_s["index_step"], step)
                    weight = stat[:, 6, m * IDX + i:m * IDX + i + 1]
                    dve.scalar_tensor_tensor(
                        out=kept[b][:], in0=sm[i][:, 0:keys], scalar=weight,
                        in1=kept[b][:] if i else causal[:, T - keys:], op0=MULT, op1=ADD).then_inc(od_s["index_step"], 1)
                    step += 1

            def rounds_before(u):
                return FIRST_ROUNDS + u

            chosen = [0]

            def do(ins):
                chosen[0] += 1
                ins.then_inc(od_s["sel_step"], 1)
                dve.wait_ge(od_s["sel_step"], chosen[0])

            def select(number):
                if number >= ROUNDS * len(CHOOSING):
                    return
                b, at = divmod(number, ROUNDS)
                keys = (CHOOSING[b] + 1) * QB
                scores, rest, pre = kept[b][:], work[:, 0:keys], widx[:, 0:keys]
                top = stat[:, 7, 0:8]
                src = rest if at else scores
                if number == 0:
                    dve.wait_ge(od_s["index_step"], len(CHOOSING) * IDX)
                do(dve.max(out=top, in_=src))
                if at < ROUNDS - 1:
                    do(dve.match_replace(out=rest, in_to_replace=top, in_values=src,
                                         imm_value=LOWEST))
                    return
                last, count = stat[:, 7, 7:8], stat[:, 7, 8:9]
                do(dve.tensor_scalar(rest, scores, last, 0.0, ALU.is_gt, ADD, accum_out=count))
                do(dve.tensor_scalar(scores, scores, last, None, ALU.is_equal))
                do(dve.tensor_scalar(count, count, -1.0, float(KEEP), MULT, ADD))
                do(dve.tensor_tensor_scan(pre, scores, scores, 0.0, ADD, ALU.max))
                do(dve.scalar_tensor_tensor(out=scores, in0=pre, scalar=count, in1=scores,
                                            op0=ALU.is_le, op1=MULT))
                do(dve.tensor_tensor(rest, rest, scores, ADD))
                do(dve.tensor_scalar(scores, rest, -MASKED, MASKED, MULT, ADD))

            def mask(u):
                kind, m, hh = UNITS[u]
                keys = (m + 1) * QB
                for s in JOBS_OF[u]:
                    dve.wait_ge(od_s["scores"], s + 1)
                    if s >= len(sm):
                        dve.wait_ge(od_s["turned"], UNIT_OF[s - len(sm)] + 1)
                    added = kept[m - CHOOSING[0]][:] if kind == "c" and m in CHOOSING \
                        else causal[:, T - keys:]
                    dve.tensor_tensor_reduce(
                        out=sm[s % len(sm)][:, 0:keys], in0=ps[:, s % 3, 0:keys], in1=added,
                        scale=1.0, scalar=LOWEST, op0=ADD, op1=ALU.max,
                        accum_out=job[:, 0, s:s + 1]).then_inc(od_s["masked"], 1)
                for s in JOBS_OF[u]:
                    dve.wait_ge(od_s["masked"], s + 1)
                    dve.tensor_scalar(job[:, 1, s:s + 1], job[:, 0, s:s + 1], -SCALE, None, MULT)\
                       .then_inc(od_s["bias"], 1)

            def recip(u):
                for s in JOBS_OF[u]:
                    dve.wait_ge(od_s["exp"], s + 1)
                    dve.reciprocal(job[:, 3, s:s + 1], job[:, 2, s:s + 1]).then_inc(od_s["recip"], 1)

            def combine(u):
                if UNITS[u][0] != "d":
                    return
                keys = (UNITS[u][1] + 1) * QB
                s, t = JOBS_OF[u]
                dve.wait_ge(od_s["recip"], t + 1)
                do(dve.tensor_tensor(job[:, 3, t:t + 1], job[:, 3, t:t + 1], sc[:, LAM, 2:3], MULT))
                dve.wait_ge(od_s["scaled"], u + 1)
                one, two = sm[s % len(sm)][:, 0:keys], sm[t % len(sm)][:, 0:keys]
                dve.scalar_tensor_tensor(out=one, in0=two, scalar=job[:, 3, t:t + 1], in1=one,
                                         op0=MULT, op1=ADD).then_inc(od_s["normed"], 1)

            def out_lo(m):
                dve.wait_ge(od_s["c_hi"], m + 1)
                span = [a[:, 0:4 * T].rearrange("p (i t) -> p i t", i=4)[:, :, m * QB:(m + 1) * QB]
                        for a in (act_hi, act_lo)]
                dve.tensor_tensor(span[1], ps[:, 5 + m % 2].rearrange("p (i q) -> p i q", i=4),
                                  span[0].bitcast(F32), SUB).then_inc(od_s["c_lo"], 1)

            for number in range(FIRST_ROUNDS):
                select(number)
            mask(0)
            mask(1)
            recip(0)
            combine(0)
            for u in range(len(UNITS)):
                if u + 2 < len(UNITS):
                    mask(u + 2)
                if u + 1 < len(UNITS):
                    recip(u + 1)
                for number in range(rounds_before(u), rounds_before(u + 1)):
                    select(number)
                if u + 1 < len(UNITS):
                    combine(u + 1)
                kind, m, hh = UNITS[u]
                if kind == "c" and hh == 0 and m:
                    out_lo(m - 1)
                if u == NORM_AT + 6:
                    dve.wait_ge(od_s["d_std"], 1)
                    dve.reciprocal(stat[:, 5], stat[:, 4]).then_inc(od_s["d_rstd"], 1)
                if u - NORM_AT - 8 in range(4):
                    i = u - NORM_AT - 8
                    dve.wait_ge(od_s["d_spread"], i + 1)
                    dve.scalar_tensor_tensor(out=od[:, i], in0=od[:, i], scalar=sc[:, LAM, 3:4],
                                             in1=ps[:, 7], op0=MULT, op1=MULT)\
                       .then_inc(od_s["d_out"], 1)
                if u - NORM_AT - 10 in range(4):
                    i = u - NORM_AT - 10
                    dve.wait_ge(od_s["d_hi"], i + 1)
                    span = slice((4 + i) * T, (5 + i) * T)
                    dve.tensor_tensor(act_lo[:, span], od[:, i], act_hi[:, span].bitcast(F32), SUB)\
                       .then_inc(od_s["d_lo"], 1)
            out_lo(NQ - 1)

        @block.vector
        def _(dve):
            dve.wait_ge(s5_loaded, 16)
            s5_angles_dve(dve)
            dve.wait_ge(gains_loaded, 16)
            split_lo(dve, 0, 0)
            for k in range(KD):
                if k == 4:
                    split_lo(dve, 0, 1)
                gained_lo(dve, 0, k)
            ffn_up_dve(dve, 0, 0, STARTS[0])
            down_dve(dve, 1, STARTS[0] + FFN_UP, NF // 2, 0, 0.5,
                     beside=S5_BESIDE)
            ev_in_dve(dve, 1, STARTS[1])
            ev_dve(dve)
            down_dve(dve, 2, STARTS[2], EV_OUT // 2, 1, 1.0)
            ffn_up_dve(dve, 1, 2, STARTS[3])
            down_dve(dve, 3, STARTS[3] + FFN_UP, NF // 2, 2, 0.5, lambda v: embedding_lo(v, 0))
            ple_dve(dve, 0, 3, STARTS[4])
            ffn_up_dve(dve, 2, 4, STARTS[5])
            down_dve(dve, 5, STARTS[5] + FFN_UP, NF // 2, 3, 0.5)
            od_dve(dve)
            down_dve(dve, 6, STARTS[7], OD_OUT // 2, 4, 1.0)
            ffn_up_dve(dve, 3, 6, STARTS[8])
            down_dve(dve, 7, STARTS[8] + FFN_UP, NF // 2, 5, 0.5, lambda v: embedding_lo(v, 1))
            ple_dve(dve, 1, 7, STARTS[9])
            reciprocal_root(dve, 8)
            for k in range(KD):
                dve.scalar_tensor_tensor(out=result[:, k], in0=h[:, k], scalar=gains[:, 8, k:k + 1],
                                         in1=rstd[:], op0=MULT, op1=MULT).then_inc(out_ready, 1)

        @block.sync
        def _(sp):
            sp.dma_start(s5_par[:], A["s5_par"]).then_inc(s5_loaded, 16)
            sp.dma_start(gains[:], A["gains"]).then_inc(gains_loaded, 16)
            x_rows = A["xT"].rearrange("(k p) t -> p k t", p=P)
            for slot in range(SLOTS):
                sp.dma_start(raw[:, slot], A["weights"][slot]).then_inc(raw_loaded[slot], 16)
                for i in (0, 1) if slot == 0 else (2, 3) if slot == 1 else ():
                    sp.dma_start(h[:, 2 * i:2 * i + 2], x_rows[:, 2 * i:2 * i + 2])\
                      .then_inc(h_loaded[i], 16)
                if slot == 1:
                    sp.dma_start(params[:], A["params"]).then_inc(param_loaded, 16)
                    sp.dma_start(sc[:, SINKS], A["sinks"]).then_inc(param_loaded, 16)
            turns = CHUNKS // SLOTS
            with sp.Fori(1, turns, 1) as i:
                for slot in range(SLOTS):
                    sp.wait_ge(split_ready, i * SLOTS + (slot - SLOTS + 1))
                    sp.dma_start(raw[:, slot], A["weights"][bass.ds(i * SLOTS + slot, 1)]
                                 .rearrange("a p b f -> (a p) b f")).then_inc(raw_loaded[slot], 16)
            for c in range(turns * SLOTS, CHUNKS):
                sp.wait_ge(split_ready, c - SLOTS + 1)
                sp.dma_start(raw[:, c % SLOTS], A["weights"][c]).then_inc(raw_loaded[c % SLOTS], 16)
            rows = out.rearrange("(k p) t -> p k t", p=P)
            for k in range(0, KD, 2):
                sp.wait_ge(out_ready, k + 2)
                sp.dma_start(rows[:, k:k + 2], result[:, k:k + 2]).then_inc(stored, 16)
            sp.wait_ge(stored, 16 * KD // 2)

        def sum_squares(pool, n):
            done = SUM_STEPS * n
            for k in range(KD):
                if n == 0:
                    pool.wait_ge(h_loaded[k // 2], 16)
                else:
                    pool.wait_ge(h_ready, tiles_before(n, k))
                if k == 0:
                    if n > 0:
                        pool.wait_ge(ssq_ready, n)
                    pool.tensor_tensor(sumsq[:], h[:, 0], h[:, 0], MULT).then_inc(sum_step, 1)
                    done += 1
                    continue
                pool.tensor_tensor(square[:, k % 2], h[:, k], h[:, k], MULT).then_inc(sum_step, 1)
                pool.wait_ge(sum_step, done + 1)
                pool.tensor_tensor(sumsq[:], sumsq[:], square[:, k % 2], ADD).then_inc(sum_step, 1)
                done += 2
                pool.wait_ge(sum_step, done)

        def s5_loads(pool):
            for dst, name in ((b_re, "s5_b_re"), (b_im, "s5_b_im"), (c0_re, "s5_c_re"),
                              (c0_im, "s5_c_im")):
                pool.dma_start(dst[:], A[name]).then_inc(tab_in, 16)

        def s5_outputs_pool(pool):
            steps = [0]

            def do(o, a, b, op):
                steps[0] += 1
                pool.tensor_tensor(o, a, b, op).then_inc(tab_c, 1)
                pool.wait_ge(tab_c, steps[0])

            pool.wait_ge(tab_in, 64)
            pool.wait_ge(tab, TAB["powers"])
            for s in range(S5_L):
                cmul(do, (m_c, m_d), c_re[:, :, :, s], c_im[:, :, :, s], c0_re[:], c0_im[:],
                     *power(s + 1), FULL, -1)
            do(c0_im[:], c0_im[:], minus[:, 0:1].unsqueeze(2).to_broadcast(FULL), MULT)
            TAB["outputs"] = steps[0]

        def ev_pool(pool):
            pool.memset(k_pad[:, 0:CH], 0.0).then_inc(pads_ready, 1)
            pool.memset(v_pad[:, 0:CH], 0.0).then_inc(pads_ready, 1)
            pool.memset(neg_row[:], 0.0).then_inc(pads_ready, 1)
            pool.wait_ge(pads_ready, 3)
            pool.memset(neg_row[:, 0:CH], MASKED).then_inc(pads_ready, 1)
            pool.memset(s_re[:, :, 0:1], 0.0).then_inc(pads_ready, 1)
            pool.memset(s_im[:, :, 0:1], 0.0).then_inc(pads_ready, 1)
            s5_outputs_pool(pool)
            pool.wait_ge(tab_pe, 4)
            pool.memset(placed[:], 0.0).then_inc(tab_zero, 1)
            pool.wait_ge(chunk_used, STARTS[2])
            pool.dma_start(w_glu[:], A["w_glu"]).then_inc(tab_in, 16)
            for m in range(NQ):
                pool.wait_ge(ev["recip"], m + 1)
                pool.tensor_tensor(prob[:, m % 2], prob[:, m % 2],
                                   stat[:, 4 + m % 2, 0:HEADS].unsqueeze(2)
                                   .to_broadcast([P, HEADS, P]), MULT).then_inc(ev["normed"], 1)

        def load_embedding(pool, layer, segment):
            pool.wait_ge(chunk_used, STARTS[segment + 1] - NF // 2 + 3)
            pool.dma_start(p_raw[:], A["pT"][layer].rearrange("(k p) t -> p k t", p=P))\
                .then_inc(p_loaded, 16)

        def od_pool(pool):
            pool.wait_ge(chunk_used, STARTS[6])
            for dst, name in ((w_uq, "w_uq"), (w_qidx, "w_qidx"), (w_uk, "w_uk"), (w_uv, "w_uv"),
                              (lam_vec, "lam_vec")):
                pool.dma_start(dst[:], A[name]).then_inc(od_s["w_loaded"], 16)
            pool.memset(causal[:], 0.0).then_inc(od_s["const"], 1)
            pool.wait_ge(od_s["const"], 1)
            pool.memset(causal[0:CH, T - CH:], MASKED).then_inc(od_s["const"], 1)
            zb = z_base(5)
            pool.wait_ge(z_ready, zb + 3)
            pool.tensor_tensor(sm[0][:], cq[:, 0], cq[:, 0], MULT).then_inc(od_s["sq_step"], 1)
            pool.tensor_tensor(sm[1][:], cq[:, 1], cq[:, 1], MULT).then_inc(od_s["sq_step"], 1)
            pool.tensor_tensor(sm[2][:], ckv[:], ckv[:], MULT).then_inc(od_s["sq_step"], 1)
            pool.wait_ge(od_s["sq_step"], 3)
            pool.tensor_tensor(sm[0][:], sm[0][:], sm[1][:], ADD).then_inc(od_s["sq_step"], 1)
            for u, (kind, m, hh) in enumerate(UNITS):
                s = JOBS_OF[u][0]
                keys = (m + 1) * QB
                pool.wait_ge(od_s["recip"], s + 1)
                pool.tensor_scalar(sm[s % len(sm)][:, 0:keys], sm[s % len(sm)][:, 0:keys],
                                   job[:, 3, s:s + 1], None, MULT).then_inc(od_s["scaled"], 1)
                if u - NORM_AT in range(4):
                    i = u - NORM_AT
                    pool.wait_ge(od_s["d_copied"], NQ)
                    pool.tensor_tensor(sq_d[:, i], od[:, i], od[:, i], MULT)\
                        .then_inc(od_s["d_sq"], 1)
                if u - NORM_AT - 7 in range(4):
                    i = u - NORM_AT - 7
                    pool.wait_ge(od_s["d_rstd"], 1)
                    blocks = [P, NQ, QB]
                    pool.tensor_tensor(sq_d[:, i].rearrange("p (m q) -> p m q", m=NQ),
                                       ident[:].unsqueeze(1).to_broadcast(blocks),
                                       stat[:, 5, NQ * i:NQ * i + NQ].unsqueeze(2)
                                       .to_broadcast(blocks), MULT).then_inc(od_s["d_diag"], 1)

        @block.gpsimd
        def _(pool):
            pool.memset(eps[:], EPS).then_inc(const_ready, 1)
            pool.memset(ones[:], 1.0).then_inc(const_ready, 1)
            pool.memset(minus[:], -1.0).then_inc(const_ready, 1)
            pool.memset(ident[:], 0.0).then_inc(const_ready, 1)
            pool.wait_ge(const_ready, 4)
            pool.affine_select(out=ident[:], in_=ident[:], compare_op=ALU.not_equal, fill=1.0,
                               base=0, pattern=[[-1, P]], channel_multiplier=1)\
                .then_inc(const_ready, 1)
            sum_squares(pool, 0)
            sum_squares(pool, 1)
            pool.wait_ge(chunk_used, STARTS[1])
            s5_loads(pool)
            ev_pool(pool)
            sum_squares(pool, 2)
            load_embedding(pool, 0, 3)
            sum_squares(pool, 3)
            sum_squares(pool, 4)
            sum_squares(pool, 5)
            od_pool(pool)
            sum_squares(pool, 6)
            load_embedding(pool, 1, 8)
            sum_squares(pool, 7)
            sum_squares(pool, 8)

        def root(act, n):
            act.wait_ge(ssq_ready, n + 1)
            act.activation(std[:], ps[:, 3 if n in (3, 7) else 4], ACT.Sqrt, bias=eps[:, 0:1],
                           scale=1.0 / D).then_inc(std_ready, 1)

        def gained_hi(act, n, k):
            if n == 0:
                act.wait_ge(h_loaded[k // 2], 16)
            else:
                act.wait_ge(h_ready, tiles_before(n, k))
            act.activation(x_hi[:, k], h[:, k], ACT.Copy, scale=gains[:, n, k:k + 1])\
               .then_inc(x_hi_ready, 1)

        def ffn_up_act(act, f, n, first):
            s = ffn_sems[f]

            def silu(tile, b):
                act.wait_ge(s["gate_scaled"], tile + 1)
                act.activation(t1[:, b], t1[:, b], ACT.Silu).then_inc(s["silu_done"], 1)

            def product_hi(tile, b):
                act.wait_ge(s["prod_done"], tile + 1)
                act.activation(act_hi[:, bass.ds(tile * T, T)], t2[:, b], ACT.Copy)\
                   .then_inc(s["act_hi_ready"], 1)

            def two_tiles(i, peeled=False):
                split_hi(act, first, AHEAD, i)
                split_hi(act, first, AHEAD + 1, i)
                if peeled:
                    root(act, n)
                silu(i * 2, 0)
                split_hi(act, first, AHEAD + 2, i)
                product_hi(i * 2, 0)
                split_hi(act, first, AHEAD + 3, i)
                silu(i * 2 + 1, 1)
                product_hi(i * 2 + 1, 1)

            two_tiles(0, peeled=True)
            with act.Fori(1, NF // 2, 1) as i:
                two_tiles(i)

        def down_act(act, n, first, steps, after=None):
            loops = steps // 4
            if loops > 1:
                with act.Fori(0, loops, 1) as i:
                    for j in range(4):
                        split_hi(act, first, AHEAD + j, i)
            else:
                loops = 0
            for j in range(4 * loops, steps):
                split_hi(act, first, AHEAD + j)
            for j in range(steps):
                split_hi(act, first, AHEAD + steps + j)
                if j < GROUP and n < NORMS - 1:
                    gained_hi(act, n, j)
                if after and j == AFTER:
                    after(act)
            if n < NORMS - 1:
                for k in range(min(steps, GROUP), KD):
                    gained_hi(act, n, k)

        def embedding_hi(act, layer):
            act.wait_ge(p_loaded, 16 * (layer + 1))
            act.activation(p_hi[:], p_raw[:], ACT.Copy).then_inc(p_hi_ready, 1)

        def ple_act(act, layer, n, first):
            for j, what in enumerate(PLE_ORDER):
                if what != "G1":
                    split_hi(act, first, AHEAD + j)
                if what[0] == "G":
                    k = int(what[1])
                    if k == 0:
                        split_hi(act, first, AHEAD + j + 1)
                        root(act, n)
                    if k == KD - 1 and n + 1 < NORMS - 1:
                        act.wait_ge(chunk_used, first + len(PLE_ORDER))
                        gained_hi(act, n + 1, 0)
                    act.wait_ge(ple_scaled, KD * layer + k + 1)
                    act.activation(t1[:, k % 2], t1[:, k % 2], ACT.Sigmoid).then_inc(ple_gate, 1)
            if n + 1 < NORMS - 1:
                for k in range(1, KD):
                    gained_hi(act, n + 1, k)

        def s5_turned_act(act):
            for half in range(4):
                act.wait_ge(tab_pe, half + 1)
                dst = (w_re, w_im)[half // 2]
                act.activation(dst[:, 4 * (half % 2):4 * (half % 2) + 4],
                               ps[:, 4 + half].rearrange("p (j q) -> p j q", j=4), ACT.Copy)\
                   .then_inc(tab_act, 1)

        def s5_taps_act(act):
            act.wait_ge(tab_pe, 5)
            act.activation(taps[:], ps[0:S5_P, 4:8].rearrange("p b (g x) -> p (b g) x", g=4),
                           ACT.Copy).then_inc(tab_taps, 1)
            act.wait_ge(tab_zero, 1)
            act.wait_ge(tab_taps, 1)
            flat = placed[:].rearrange("p g s q -> p g (s q)")
            for s in range(S5_L):
                act.dma_start(flat[s::S5_L, :, s * S5_P:],
                              taps[:, :, 0:(S5_L - s) * S5_P]).then_inc(tab_moved, 16)

        def ev_in_act(act, n, first):
            for j in range(EV_IN):
                if j != 1:
                    split_hi(act, first, AHEAD + j)
                if j == 0:
                    split_hi(act, first, AHEAD + 1)
                    root(act, n)
                if j in (2, 3):
                    act.wait_ge(z_ready, j - 1)
                    act.activation(u_sc[:, j - 2],
                                   u_ch[:, j - 2].rearrange("p (c s) -> p s c", s=S5_L), ACT.Copy)\
                       .then_inc(u_sorted, 1)
                if j == 3:
                    act.wait_ge(u_sorted, S5_T)
                    act.dma_start(scratch_u.rearrange("(t p) s c -> p t s c", t=S5_T), u_sc[:])\
                       .then_inc(u_moved, 16)
                if j == 5:
                    act.wait_ge(u_moved, 16)
                    act.dma_start(u_grp[:], scratch_u.rearrange("(g p) s c -> (p s) g c", g=S5_G))\
                       .then_inc(u_moved, 16)
                if j == 6:
                    s5_turned_act(act)

        def ev_act(act):

            def exps(m):
                act.wait_ge(ev["bias"], m + 1)
                if m >= 2:
                    act.wait_ge(ev["turned"], m - 1)
                for hh in range(HEADS):
                    act.activation(prob[:, m % 2, hh],
                                   ps[:, 2 * (m % 2) + hh // 4, (hh % 4) * P:(hh % 4 + 1) * P],
                                   ACT.Exp, bias=stat[:, m % 2, hh:hh + 1], scale=SCALE,
                                   accum_out=stat[:, 2 + m % 2, hh:hh + 1]).then_inc(ev["exp"], 1)
                act.activation(stat[:, 6 + m % 2, 0:HEADS], stat[:, 6 + m % 2, 0:HEADS], ACT.Exp)\
                   .then_inc(ev["sink_exp"], 1)

            def turned(m):
                act.wait_ge(ev["turned"], m + 1)
                if m == 0:
                    act.wait_ge(tab_moved, 16 * S5_L)
                act.activation(prob_t[:, m % 2], ps[:, 4:6].rearrange("p b (h q) -> p (b h) q", h=4),
                               ACT.Copy).then_inc(ev["turned_copied"], 1)

            def out_hi(m):
                act.wait_ge(ev["pv"], m + 1)
                act.activation(act_hi[:, 0:4 * T].rearrange("p (i t) -> p i t", i=4)
                               [:, :, m * QB:(m + 1) * QB],
                               ps[:, 6].rearrange("p (i q) -> p i q", i=4), ACT.Copy)\
                   .then_inc(ev["hi"], 1)

            exps(0)
            s5_taps_act(act)
            act.wait_ge(ev["v_turned"], 1)
            act.activation(v_band[:], ps[:, 4:6].rearrange("p b (n x) -> p (b n) x", n=4), ACT.Copy)\
               .then_inc(ev["v_ready"], 1)
            exps(1)
            turned(0)
            act.wait_ge(s5["y_done"], 1)
            act.activation(y_grp[:], ps[:, 6:8].rearrange("p b (g c) -> p (b g) c", g=8), ACT.Copy)\
               .then_inc(s5["y_copied"], 1)
            act.wait_ge(s5["y_copied"], 1)
            rows = scratch_y.rearrange("(j two p) s c -> two (p s) j c", two=2, p=S5_P)
            for parity in range(2):
                act.dma_start(rows[parity], y_grp[:, S5_J * parity:S5_J * (parity + 1)])\
                   .then_inc(y_moved, 16)
            exps(2)
            turned(1)
            out_hi(0)
            act.wait_ge(y_moved, 32)
            act.dma_start(y_ch[:], scratch_y.rearrange("(t p) s c -> p t (s c)", t=S5_T))\
               .then_inc(y_moved, 16)
            exps(3)
            turned(2)
            out_hi(1)
            turned(3)
            out_hi(2)
            out_hi(3)
            act.wait_ge(s5["skip_done"], S5_T)
            act.activation(y_act[:], y_act[:], ACT.Gelu_apprx_tanh).then_inc(s5["gelu_done"], 1)
            for t in range(S5_T):
                act.wait_ge(s5["glu_done"], t + 1)
                if t == 0:
                    act.wait_ge(y_moved, 32)
                act.activation(glu[:, t], ps[:, t], ACT.Sigmoid).then_inc(s5["gate_ready"], 1)
            for t in range(S5_T):
                act.wait_ge(s5["prod_done"], t + 1)
                act.activation(act_hi[:, (4 + t) * T:(5 + t) * T], glu[:, t], ACT.Copy)\
                   .then_inc(s5["hi_ready"], 1)

        def block_out(act, kind, m):
            unit = UNITS.index((kind, m, 3 if kind == "d" else HEADS - 1))
            act.wait_ge(od_s["pv"], unit + 1)
            src = ps[:, 5 + m % 2].rearrange("p (i q) -> p i q", i=4)
            if kind == "d":
                act.activation(od[:, :, m * QB:(m + 1) * QB], src, ACT.Copy)\
                   .then_inc(od_s["d_copied"], 1)
            else:
                act.activation(act_hi[:, 0:4 * T].rearrange("p (i t) -> p i t", i=4)
                               [:, :, m * QB:(m + 1) * QB], src, ACT.Copy).then_inc(od_s["c_hi"], 1)

        def od_act(act):
            first = STARTS[6]
            for j in range(OD_IN):
                if j != 1:
                    split_hi(act, first, AHEAD + j)
                if j == 0:
                    split_hi(act, first, AHEAD + 1)
                    root(act, 5)
                if j == 7:
                    act.wait_ge(od_s["ssq"], 2)
                    for i, width in enumerate((2 * P, P)):
                        act.activation(sm[3 + i][:], ps[:, 5 + i], ACT.Sqrt, bias=eps[:, 0:1],
                                       scale=1.0 / width).then_inc(od_s["std"], 1)
            act.wait_ge(od_s["lam"], 2)
            act.activation(sc[:, LAM, 0:2], sc[:, LAM, 0:2], ACT.Exp).then_inc(od_s["lam"], 1)
            for number, (kind, i, bank) in enumerate(PREP):
                act.wait_ge(od_s["prep"], number + 1)
                if kind == "weight":
                    last = act.activation(stat[:, 6, 0:NQ * IDX], ps[:, bank, 0:NQ * IDX], ACT.Copy,
                                          scale=IDX ** -0.5)
                elif kind == "index":
                    keys = (i // IDX + 1) * QB
                    if i // IDX > CHOOSING[0]:
                        act.wait_ge(od_s["index_step"], i - (CHOOSING[0] + 1) * IDX + 1)
                    last = act.activation(sm[i % IDX][:, 0:keys], ps[:, bank, 0:keys], ACT.Relu,
                                          scale=HD ** -0.5)
                else:
                    dst = {"q_idx": q_idx, "q": q_t, "k": k_t, "v": v_h, "dv": v_d}[kind]
                    last = act.activation(dst[:, i], ps[:, bank], ACT.Copy)
                last.then_inc(od_s["prep_read"], 1)

            def exps(u):
                keys = (UNITS[u][1] + 1) * QB
                for s in JOBS_OF[u]:
                    act.wait_ge(od_s["bias"], s + 1)
                    buf = sm[s % len(sm)][:, 0:keys]
                    act.activation(buf, buf, ACT.Exp, bias=job[:, 1, s:s + 1], scale=SCALE,
                                   accum_out=job[:, 2, s:s + 1]).then_inc(od_s["exp"], 1)

            def turned(u):
                keys = (UNITS[u][1] + 1) * QB
                act.wait_ge(od_s["turned"], u + 1)
                if u >= 2:
                    act.wait_ge(od_s["pv"], u - 1)
                act.activation(pt[:, u % 2, 0:keys], ps[:, 3 + u % 2, 0:keys], ACT.Copy)\
                   .then_inc(od_s["turned_copied"], 1)

            exps(0)
            exps(1)
            for u, (kind, m, hh) in enumerate(UNITS):
                if u + 2 < len(UNITS):
                    exps(u + 2)
                turned(u)
                if u and UNITS[u - 1][:2] != (kind, m):
                    block_out(act, *UNITS[u - 1][:2])
                if u == NORM_AT + 6:
                    act.wait_ge(od_s["d_ssq"], 4)
                    act.activation(stat[:, 4], ps[:, 7, 0:16], ACT.Sqrt, bias=eps[:, 0:1],
                                   scale=1.0 / P).then_inc(od_s["d_std"], 1)
                if u - NORM_AT - 9 in range(4):
                    i = u - NORM_AT - 9
                    act.wait_ge(od_s["d_out"], i + 1)
                    act.activation(act_hi[:, (4 + i) * T:(5 + i) * T], od[:, i], ACT.Copy)\
                       .then_inc(od_s["d_hi"], 1)
            block_out(act, "c", NQ - 1)

        @block.scalar
        def _(act):
            act.wait_ge(gains_loaded, 16)
            act.wait_ge(const_ready, 5)
            act.wait_ge(tab, TAB["angles"])
            act.activation(sc[:, SIN:SIN + 4], sc[:, SIN:SIN + 4], ACT.Sin).then_inc(tab_act, 1)
            split_hi(act, 0, 0)
            for k in range(KD):
                if k == 4:
                    split_hi(act, 0, 1)
                gained_hi(act, 0, k)
            ffn_up_act(act, 0, 0, STARTS[0])
            down_act(act, 1, STARTS[0] + FFN_UP, NF // 2)
            ev_in_act(act, 1, STARTS[1])
            ev_act(act)
            down_act(act, 2, STARTS[2], EV_OUT // 2)
            ffn_up_act(act, 1, 2, STARTS[3])
            down_act(act, 3, STARTS[3] + FFN_UP, NF // 2, lambda a: embedding_hi(a, 0))
            ple_act(act, 0, 3, STARTS[4])
            ffn_up_act(act, 2, 4, STARTS[5])
            down_act(act, 5, STARTS[5] + FFN_UP, NF // 2)
            od_act(act)
            down_act(act, 6, STARTS[7], OD_OUT // 2)
            ffn_up_act(act, 3, 6, STARTS[8])
            down_act(act, 7, STARTS[8] + FFN_UP, NF // 2, lambda a: embedding_hi(a, 1))
            ple_act(act, 1, 7, STARTS[9])
            root(act, 8)

        def in_chunk(pe, first, j, bank, i=0, n=None, rhs=(x_hi, x_lo)):
            slot = slot_of(first, j)
            pe.wait_ge(split_ready, i * 4 + (first + j + 1))
            if n:
                pe.wait_ge(h_ready, tiles_before(n, GROUP))
            for k in range(KD):
                if n is not None:
                    pe.wait_ge(x_lo_ready, KD * n + k + 1)
                for part, (w, x) in enumerate(((w_hi, rhs[0]), (w_hi, rhs[1]), (w_lo, rhs[0]))):
                    last = pe.matmul(ps[:, bank], w[:, slot, k], x[:, k],
                                     start=(k == 0 and part == 0), stop=(k == KD - 1 and part == 2))
            last.then_inc(chunk_used, 1)

        def down_chunk(pe, first, j, group, start, stop_, rhs_hi, rhs_lo, i=0, whole=True):
            slot = slot_of(first, j)
            pe.wait_ge(split_ready, i * 4 + (first + j + 1))
            for d in range(GROUP):
                for row in range(2):
                    b = row * GROUP + d
                    for part, (w, x) in enumerate(((w_hi, rhs_hi), (w_hi, rhs_lo), (w_lo, rhs_hi))):
                        last = pe.matmul(ps[:, (4, 0)[group] + d], w[:, slot, b], x(row),
                                         start=(start and row == 0 and part == 0),
                                         stop=(stop_ and row == 1 and part == 2))
                if stop_ and d < GROUP - 1 and whole:
                    last.then_inc(tile_done, 1)
            last.then_inc(chunk_used, 1)

        def squares(pe, n):
            pe.wait_ge(sum_step, SUM_STEPS * (n + 1))
            pe.matmul(ps[:, 3 if n in (3, 7) else 4], ones[:], sumsq[:], start=True, stop=True)\
              .then_inc(ssq_ready, 1)

        def ffn_up_pe(pe, f, n, first):
            s = ffn_sems[f]
            for j in range(4):
                in_chunk(pe, first, j, j, n=n if j == 0 else None)
                if j == 1:
                    squares(pe, n)
            with pe.Fori(1, NF // 2, 1) as i:
                for j in range(4):
                    tile = i * 2 + j // 2
                    pe.wait_ge(s["up_scaled"] if j % 2 else s["gate_scaled"], tile - 1)
                    in_chunk(pe, first, j, j, i)

        def down_pe(pe, first, steps, ready):
            for group in range(2):
                begin = first + steps * group

                def rhs(a, m):
                    return lambda row: a[:, bass.ds((m * 2 + row) * T, T)]

                def static(a, m):
                    return lambda row: a[:, (m * 2 + row) * T:(m * 2 + row + 1) * T]

                def chunk(m):
                    if group == 0:
                        ready(pe, m)
                    down_chunk(pe, begin, m, group, m == 0, m == steps - 1,
                               static(act_hi, m), static(act_lo, m))

                chunk(0)
                m = 1
                if steps > 8:
                    with pe.Fori(0, 2, 1) as i:
                        for j in range(4):
                            at = i * 4 + (1 + j)
                            if group == 0:
                                ready(pe, at)
                            down_chunk(pe, begin, 1 + j, group, False, False,
                                       rhs(act_hi, at), rhs(act_lo, at), i)
                    m = 9
                while m < steps:
                    chunk(m)
                    m += 1

        def ffn_pe(pe, f, n, first):
            ffn_up_pe(pe, f, n, first)
            pe.wait_ge(std_ready, n + 1)

            def ready(pe, m):
                pe.wait_ge(ffn_sems[f]["act_ready"], m * 2 + 2)
            down_pe(pe, first + FFN_UP, NF // 2, ready)

        def ple_pe(pe, layer, n, first):
            for j, what in enumerate(PLE_ORDER):
                k = int(what[1])
                if what[0] == "P":
                    if k == 0:
                        pe.wait_ge(p_ready, layer + 1)
                        pe.wait_ge(h_ready, tiles_before(n, GROUP - 1))
                    else:
                        pe.wait_ge(ple_term, KD * layer + GROUP)
                    slot = slot_of(first, j)
                    pe.wait_ge(split_ready, first + j + 1)
                    for d in range(GROUP):
                        for row in range(2):
                            b = row * GROUP + d
                            for part, (w, x) in enumerate(((w_hi, p_hi), (w_hi, p_lo), (w_lo, p_hi))):
                                last = pe.matmul(ps[:, 4 + d], w[:, slot, b], x[:, row],
                                                 start=(row == 0 and part == 0),
                                                 stop=(row == 1 and part == 2))
                    last.then_inc(chunk_used, 1)
                    continue
                if k == 3:
                    pe.wait_ge(std_ready, n + 1)
                if k >= GROUP:
                    pe.wait_ge(ple_scaled, KD * layer + k - GROUP + 1)
                in_chunk(pe, first, j, k % GROUP, n=n if k == 0 else None)
                if k == 1:
                    squares(pe, n)

        def z_pe(pe, n, first, tiles, extra=None):
            for j in range(tiles):
                if j >= 4:
                    pe.wait_ge(z_ready, z_base(n) + j - 3)
                in_chunk(pe, first, j, j % 4, n=n if j == 0 else None)
                if j == 1:
                    squares(pe, n)
                if extra:
                    extra(pe, j)

        def s5_turn_pe(pe, tile):
            if tile != EV_IN - 2:
                return
            pe.wait_ge(tab, TAB["inputs"])
            pe.wait_ge(std_ready, 2)
            for part, ab in enumerate((ab_re, ab_im)):
                for j in range(S5_J):
                    last = pe.transpose(ps[:, 4 + 2 * part + j // 4, (j % 4) * P:(j % 4 + 1) * P],
                                        ab[:, j].rearrange("p q s -> p (q s)"), ident[:])
                    if j % 4 == 3:
                        last.then_inc(tab_pe, 1)

        def s5_taps_pe(pe):
            pe.wait_ge(tab_c, TAB["outputs"])
            pe.wait_ge(tab_act, 5)
            for g in range(S5_G):
                j, rows = g // 2, slice(S5_N * (g % 2), S5_N * (g % 2) + S5_N)
                dst = ps[0:S5_P, 4 + 2 * (g % 2) + j // 4, (j % 4) * P:(j % 4 + 1) * P]
                first, rest = dst[:, 0:S5_P], dst[:, S5_P:]
                for part, (b, c0, c) in enumerate(((bb_re, c0_re, c_re), (bb_im, c0_im, c_im))):
                    pe.matmul(first, b[rows, j], c0[rows, j], start=(part == 0), stop=(part == 1))
                for part, (b, c0, c) in enumerate(((bb_re, c0_re, c_re), (bb_im, c0_im, c_im))):
                    last = pe.matmul(rest, b[rows, j],
                                     c[rows, j, :, 0:S5_L - 1].rearrange("p q s -> p s q"),
                                     start=(part == 0), stop=(part == 1))
            last.then_inc(tab_pe, 1)

        def ev_pe(pe):
            def scores(m):
                if m >= 2:
                    pe.wait_ge(ev["exp"], HEADS * (m - 1))
                for kv in range(2):
                    rows = slice(HD * kv, HD * kv + HD)
                    for i in range(4):
                        for half in range(2):
                            n = 2 * m + half
                            dst = ps[HD * half:HD * half + HD, 2 * (m % 2) + kv, i * P:(i + 1) * P]
                            last = pe.matmul(dst, zq[rows, i, n * CH:(n + 1) * CH],
                                             k_pad[rows, n * CH:n * CH + P], start=True, stop=n > 0)
                            if n == 0:
                                pe.matmul(dst, ones[0:1, 0:CH], neg_row[:], start=False, stop=True)
                last.then_inc(ev["scores"], 1)

            def turn(m):
                pe.wait_ge(ev["normed"], m + 1)
                if m:
                    pe.wait_ge(ev["turned_copied"], m)
                else:
                    pe.wait_ge(ev["v_ready"], 1)
                for hh in range(HEADS):
                    last = pe.transpose(ps[:, 4 + hh // 4, (hh % 4) * P:(hh % 4 + 1) * P],
                                        prob[:, m % 2, hh], ident[:])
                last.then_inc(ev["turned"], 1)

            def values(m):
                pe.wait_ge(ev["turned_copied"], m + 1)
                if m:
                    pe.wait_ge(ev["lo"], m)
                for half in range(2):
                    cols = slice(CH * half, CH * half + CH)
                    for kv in range(2):
                        rows = slice(HD * kv, HD * kv + HD)
                        last = pe.matmul(ps[rows, 6].rearrange("p (i q) -> p i q", i=4)[:, :, cols],
                                         v_band[:, 2 * m + half, rows],
                                         prob_t[:, m % 2, 4 * kv:4 * kv + 4, cols],
                                         start=True, stop=True)
                last.then_inc(ev["pv"], 1)

            pe.wait_ge(z_ready, EV_IN)
            pe.wait_ge(pads_ready, 6)
            pe.wait_ge(u_moved, 32)
            for part, w in enumerate((w_re, w_im)):
                for g in range(S5_G):
                    j, rows = g // 2, slice(S5_N * (g % 2), S5_N * (g % 2) + S5_N)
                    last = pe.matmul(ps[rows, 2 + part, j * S5_C:(j + 1) * S5_C], w[:, j, rows],
                                     u_grp[:, g], start=True, stop=True)
            last.then_inc(s5["x_done"], 1)
            scores(0)
            s5_taps_pe(pe)
            pe.wait_ge(s5["step"], TAB["x_read"])
            scores(1)
            pe.wait_ge(tab_taps, 1)
            for n in range(T // CH):
                last = pe.transpose(ps[:, 4 + n // 4, (n % 4) * P:(n % 4 + 1) * P],
                                    v_pad[:, n * CH:n * CH + P], ident[:])
            last.then_inc(ev["v_turned"], 1)
            turn(0)
            scores(2)
            pe.wait_ge(s5["state_ready"], 2)
            pe.wait_ge(tab_zero, 2)
            for g in range(S5_G):
                j, rows = g // 2, slice(S5_N * (g % 2), S5_N * (g % 2) + S5_N)
                dst = ps[:, 6 + g % 2, j * S5_C:(j + 1) * S5_C]
                pe.matmul(dst, intra[:, S5_J * (g % 2) + j], u_grp[:, g], start=True, stop=False)
                pe.matmul(dst, c_re[rows, j].rearrange("p q s -> p (q s)"), s_re[rows, j, 0:S5_C],
                          start=False, stop=False)
                last = pe.matmul(dst, c_im[rows, j].rearrange("p q s -> p (q s)"),
                                 s_im[rows, j, 0:S5_C], start=False, stop=True)
            last.then_inc(s5["y_done"], 1)
            turn(1)
            pe.wait_ge(s5["y_copied"], 1)
            values(0)
            scores(3)
            turn(2)
            values(1)
            turn(3)
            values(2)
            values(3)

        def gates_pe(pe):
            pe.wait_ge(tab_in, 80)
            pe.wait_ge(s5["gelu_done"], 1)
            pe.wait_ge(ev["exp"], HEADS * NQ)
            for t in range(S5_T):
                for k in range(S5_T):
                    last = pe.matmul(ps[:, t], w_glu[:, k, t * P:(t + 1) * P], y_act[:, k],
                                     start=(k == 0), stop=(k == S5_T - 1))
                last.then_inc(s5["glu_done"], 1)

        def od_norms_pe(pe, j):
            if j == 6:
                pe.wait_ge(od_s["sq_step"], 4)
                pe.matmul(ps[:, 5], ones[:], sm[0][:], start=True, stop=True).then_inc(od_s["ssq"], 1)
                pe.matmul(ps[:, 6], ones[:], sm[2][:], start=True, stop=True).then_inc(od_s["ssq"], 1)

        def od_pe(pe):
            pe.wait_ge(od_s["w_loaded"], 16 * 5)
            pe.wait_ge(od_s["latent"], 3)
            pe.wait_ge(z_ready, z_base(5) + OD_IN)
            pe.wait_ge(std_ready, 6)
            for number, (kind, i, bank) in enumerate(PREP):
                before = [x for x in range(number) if PREP[x][2] == bank]
                if before:
                    pe.wait_ge(od_s["prep_read"], before[-1] + 1)
                if kind == "q_idx" or kind == "q":
                    w = w_qidx if kind == "q_idx" else w_uq
                    for k in range(2):
                        last = pe.matmul(ps[:, bank], w[:, k, i * P:(i + 1) * P], cq[:, k],
                                         start=(k == 0), stop=(k == 1))
                elif kind == "weight":
                    rows = slice(HD, HD + IDX)
                    for m in range(NQ):
                        last = pe.transpose(ps[:, bank, m * IDX:(m + 1) * IDX],
                                            widx[rows, m * QB:(m + 1) * QB], ident[rows, rows])
                elif kind == "index":
                    m, head = divmod(i, IDX)
                    rows = slice(HD * (head % 2), HD * (head % 2) + HD)
                    pe.wait_ge(od_s["prep_read"], PREP.index(("q_idx", 1, 2)) + 1)
                    last = pe.matmul(ps[:, bank, 0:(m + 1) * QB],
                                     q_idx[rows, head // 2, m * QB:(m + 1) * QB],
                                     kidx[rows, 0:(m + 1) * QB], start=True, stop=True)
                elif kind == "k":
                    last = pe.matmul(ps[:, bank], w_uk[:, i * P:(i + 1) * P], ckv[:],
                                     start=True, stop=True)
                elif kind == "v":
                    last = pe.matmul(ps[:, bank], ckv[:, i * QB:(i + 1) * QB], w_uv[:],
                                     start=True, stop=True)
                else:
                    for head in range(4):
                        last = pe.transpose(ps[:, bank, head * P:(head + 1) * P],
                                            dv[:, head, i * QB:(i + 1) * QB], ident[:])
                last.then_inc(od_s["prep"], 1)

            def scores(u):
                kind, m, hh = UNITS[u]
                queries, keys = slice(m * QB, (m + 1) * QB), (m + 1) * QB
                for n, s in enumerate(JOBS_OF[u]):
                    if s >= 3:
                        pe.wait_ge(od_s["masked"], s - 2)
                    half = n if kind == "d" else hh % 2
                    rows = slice(HD * half, HD * half + HD)
                    if kind == "d":
                        lhs, rhs = dq[rows, hh, queries], dk[rows, hh, 0:keys]
                    else:
                        lhs, rhs = q_t[rows, hh // 2, queries], k_t[rows, hh // 2, 0:keys]
                    pe.matmul(ps[:, s % 3, 0:keys], lhs, rhs, start=True, stop=True)\
                      .then_inc(od_s["scores"], 1)

            def turn(u):
                kind, m, hh = UNITS[u]
                s = JOBS_OF[u][0]
                if kind == "d":
                    pe.wait_ge(od_s["normed"], u + 1)
                else:
                    pe.wait_ge(od_s["scaled"], u + 1)
                if u >= 2:
                    pe.wait_ge(od_s["turned_copied"], u - 1)
                for kb in range(m + 1):
                    last = pe.transpose(ps[:, 3 + u % 2, kb * QB:(kb + 1) * QB],
                                        sm[s % len(sm)][:, kb * QB:(kb + 1) * QB], ident[:])
                last.then_inc(od_s["turned"], 1)

            def values(u):
                kind, m, hh = UNITS[u]
                pe.wait_ge(od_s["turned_copied"], u + 1)
                if hh == 0:
                    if kind == "d" and m >= 2:
                        pe.wait_ge(od_s["d_copied"], m - 1)
                    if kind == "c" and m < 2:
                        pe.wait_ge(od_s["d_copied"], NQ - 1 + m)
                    if kind == "c" and m >= 2:
                        pe.wait_ge(od_s["c_lo"], m - 1)
                for kb in range(m + 1):
                    if kind == "d":
                        dst = ps[:, 5 + m % 2, hh * QB:(hh + 1) * QB]
                        lhs = v_d[:, kb, hh * P:(hh + 1) * P]
                    else:
                        rows = slice(HD * (hh % 2), HD * (hh % 2) + HD)
                        dst = ps[rows, 5 + m % 2, (hh // 2) * QB:(hh // 2 + 1) * QB]
                        lhs = v_h[:, kb, hh * HD:(hh + 1) * HD]
                    last = pe.matmul(dst, lhs, pt[:, u % 2, kb * QB:(kb + 1) * QB],
                                     start=(kb == 0), stop=(kb == m))
                last.then_inc(od_s["pv"], 1)

            pe.wait_ge(od_s["prep_read"], len(PREP))
            scores(0)
            scores(1)
            for u in range(len(UNITS)):
                if u + 2 < len(UNITS):
                    scores(u + 2)
                turn(u)
                if u:
                    values(u - 1)
                if u - NORM_AT - 2 in range(4):
                    i = u - NORM_AT - 2
                    pe.wait_ge(od_s["d_sq"], i + 1)
                    for b in range(NQ):
                        last = pe.matmul(ps[:, 7, NQ * i + b:NQ * i + b + 1],
                                         sq_d[:, i, b * QB:(b + 1) * QB], ones[:, 0:1],
                                         start=True, stop=True)
                    last.then_inc(od_s["d_ssq"], 1)
                if u - NORM_AT - 8 in range(4):
                    i = u - NORM_AT - 8
                    pe.wait_ge(od_s["d_diag"], i + 1)
                    if i:
                        pe.wait_ge(od_s["d_out"], i)
                    pe.matmul(ps[:, 7], ones[:], sq_d[:, i], start=True, stop=True)\
                      .then_inc(od_s["d_spread"], 1)
            values(len(UNITS) - 1)

        @block.tensor
        def _(pe):
            pe.wait_ge(const_ready, 5)
            ffn_pe(pe, 0, 0, STARTS[0])
            z_pe(pe, 1, STARTS[1], EV_IN, s5_turn_pe)
            ev_pe(pe)

            def ev_ready(pe, m):
                if m == 0:
                    pe.wait_ge(ev["lo"], NQ)
                if m == 1:
                    gates_pe(pe)
                if m == 2:
                    pe.wait_ge(s5["lo_ready"], S5_T)
            down_pe(pe, STARTS[2], EV_OUT // 2, ev_ready)
            ffn_pe(pe, 1, 2, STARTS[3])
            ple_pe(pe, 0, 3, STARTS[4])
            ffn_pe(pe, 2, 4, STARTS[5])
            z_pe(pe, 5, STARTS[6], OD_IN, od_norms_pe)
            od_pe(pe)

            def od_ready(pe, m):
                if m == 0:
                    pe.wait_ge(od_s["c_lo"], NQ)
                if m == 2:
                    pe.wait_ge(od_s["d_lo"], 4)
            down_pe(pe, STARTS[7], OD_OUT // 2, od_ready)
            ffn_pe(pe, 3, 6, STARTS[8])
            ple_pe(pe, 1, 7, STARTS[9])
            pe.wait_ge(h_ready, tiles_before(8, KD - 1))
            squares(pe, 8)



def _out_tiles(np, w):
    k, m = w.shape
    return w.reshape(k // P, P, m // P, P).transpose(2, 1, 0, 3)


def _row_pairs(np, w):
    k, m = w.shape
    a = w.reshape(k // (2 * P), 2, P, m // (GROUP * P), GROUP, P).transpose(3, 0, 2, 1, 4, 5)
    return a.reshape(-1, P, BLOCKS, P)


def _heads(np, w, axis):
    order = [i + 4 * kv for i in range(4) for kv in range(2)]
    if axis:
        return w.reshape(w.shape[0], HEADS, HD)[:, order].reshape(w.shape[0], HEADS * HD)
    return w.reshape(HEADS, HD, w.shape[1])[order].reshape(HEADS * HD, w.shape[1])


def layout(np, x):
    g = {k: np.asarray(v) for k, v in x.items()}

    def ffn(i, j):
        gate, up = (_out_tiles(np, g[n][i, j]) for n in ("ffn_w_gate", "ffn_w_up"))
        both = np.stack([gate, up], 1).reshape(-1, P, BLOCKS, P)
        return [both, _row_pairs(np, g["ffn_w_down"][i, j])]

    def ple(i):
        gate = _out_tiles(np, g["ple_w_gate"][i])
        proj = _row_pairs(np, g["ple_w_proj"][i])
        return [np.stack([(gate if w[0] == "G" else proj)[int(w[1])] for w in PLE_ORDER])]

    ev = g["ev_w_in"][0]
    nq = HEADS * HD
    ev = np.concatenate([ev[:, nq + 256:], ev[:, nq:nq + 256], _heads(np, ev[:, :nq], 1)], 1)
    ev_out = g["ev_w_out"][0]
    ev_out = np.concatenate([_heads(np, ev_out[:nq], 0), ev_out[nq:]], 0)
    od = g["od_w_in"][0]
    od = np.concatenate([od[:, :452], np.zeros((D, 60), od.dtype), od[:, 452:]], 1)
    chunks = (ffn(0, 0) + [_out_tiles(np, ev), _row_pairs(np, ev_out)] + ffn(0, 1) + ple(0)
              + ffn(1, 0) + [_out_tiles(np, od), _row_pairs(np, g["od_w_out"][0])] + ffn(1, 1)
              + ple(1))
    weights = np.concatenate(chunks, 0)

    def states(a):
        rest = a.shape[2:]
        a = a.reshape((S5_J, 2 * S5_N) + rest)
        return np.ascontiguousarray(np.moveaxis(a, 0, 1))

    log_dt = np.broadcast_to(g["s5_log_dt"][0][:, None], (S5_G, S5_N))
    params = np.zeros((P, 16), np.float32)
    params[:, 0:2] = g["s5_d"][0].reshape(2, P).T
    params[:, 2:4] = g["c_q_norm"][0].reshape(2, P).T
    params[:, 4] = g["c_kv_norm"][0]
    params[:, 5] = g["d_head_norm"][0]
    lam = np.stack([g[n][0] for n in ("d_lam_q1", "d_lam_k1", "d_lam_q2", "d_lam_k2")])
    gains = np.concatenate([g["norms"].reshape(8, D), g["final_norm"][None]], 0)
    arrays = {
        "xT": g["x"][0].T, "pT": g["p"][:, 0].transpose(0, 2, 1), "weights": weights,
        "gains": gains.reshape(NORMS, KD, P).transpose(2, 0, 1),
        "s5_par": np.stack([states(g["s5_lam_re"][0]), states(g["s5_lam_im"][0]), states(log_dt)], 1),
        "s5_b_re": states(g["s5_b_re"][0]), "s5_b_im": states(g["s5_b_im"][0]),
        "s5_c_re": states(g["s5_c_re"][0].transpose(0, 2, 1)),
        "s5_c_im": states(g["s5_c_im"][0].transpose(0, 2, 1)),
        "w_glu": g["s5_w_glu"][0].reshape(2, P, 2 * P).transpose(1, 0, 2),
        "w_uq": g["c_w_uq"][0].reshape(2, P, 4 * P).transpose(1, 0, 2),
        "w_qidx": g["c_w_qidx"][0].reshape(2, P, 2 * P).transpose(1, 0, 2),
        "w_uk": g["c_w_uk"][0].reshape(P, 4 * P), "w_uv": g["c_w_uv"][0].reshape(P, 4 * P),
        "lam_vec": np.broadcast_to(lam, (P, 4, HD)),
        "sinks": np.broadcast_to(g["a_sinks"][0], (P, HEADS)),
        "params": params,
    }
    return {k: np.ascontiguousarray(v) for k, v in arrays.items()}


def kernel(**inputs):
    import numpy as np
    import concourse.bacc as bacc
    from concourse.bass_utils import run_bass_kernel_spmd

    nc = bacc.Bacc("TRN2", target_bir_lowering=False, num_devices=1)
    arrays = layout(np, inputs)
    A = {k: nc.dram_tensor("in_" + k, v.shape, mybir.dt.from_np(v.dtype), kind="ExternalInput").ap()
         for k, v in arrays.items()}
    out = nc.dram_tensor("out", (D, T), F32, kind="ExternalOutput").ap()
    encoder(nc, A, out)
    r = run_bass_kernel_spmd(nc, [{"in_" + k: v for k, v in arrays.items()}], core_ids=[0])
    return np.ascontiguousarray(r.results[0]["out"].T).reshape(1, T, D)
```
